# Optimizing a Trainium2 kernel written in Bass

```python
import math
import jax, jax.numpy as jnp
from jax import lax
import numpy as np

D_MODEL = 1024
BATCH = 1
SEQ = 2048
DEPTH = 1
DEC_BATCH = 8
DEC_SEQ = 1
PAST_LEN = 16384
PAGE_SIZE = 128

D_MIX = D_MODEL
W_A = D_MIX // 2
H_A = 4
DH_A = W_A // H_A
W_B = D_MIX - W_A
G_B = 4
DG_B = W_B // G_B
CHUNK_B = 128
MLSTM_CHUNK = 128
CONV_W = 4
QK_W = 2 * W_A
D_IN = QK_W + 2 * W_A + 2 * H_A + 2 * W_B
SPLIT_POINTS = (QK_W, QK_W + W_A, QK_W + 2 * W_A, QK_W + 2 * W_A + H_A, QK_W + 2 * W_A + 2 * H_A, QK_W + 2 * W_A + 2 * H_A + W_B)
N_GROUPS = 4
EXPERTS_PER_GROUP = 8
N_EXPERTS = N_GROUPS * EXPERTS_PER_GROUP
TOP_K_IN_GROUP = 2
D_FF_EXPERT = D_MODEL // 2
MOE_BLOCK = 128
PLE_DIM = 256
EPS = 1e-6

kernel_name = 'hymba_mlstm_chunkmlp_hmoe_step'

def rmsnorm(x, g):
    xf = x.astype(jnp.float32)
    y = xf * lax.rsqrt(jnp.mean(xf * xf, axis=-1, keepdims=True) + EPS)
    return (y * g.astype(jnp.float32)).astype(x.dtype)

def _mlstm_chunk_step(carry, chunk):
    C, n, m = carry
    q, k, v, ig, lf = chunk
    L = q.shape[2]
    b = jnp.cumsum(lf, axis=-1)
    causal = jnp.tril(jnp.ones((L, L), dtype=bool))
    d_log = jnp.where(causal, b[..., :, None] - b[..., None, :] + ig[..., None, :], -jnp.inf)
    inter = b + m[..., None]
    m_t = jnp.maximum(inter, jnp.max(d_log, axis=-1))
    s = jnp.einsum('bhtd,bhsd->bhts', q, k) * jnp.exp(d_log - m_t[..., None])
    w_inter = jnp.exp(inter - m_t)
    num = w_inter[..., None] * jnp.einsum('bhvd,bhtd->bhtv', C, q) + jnp.einsum('bhts,bhsv->bhtv', s, v)
    nq = w_inter * jnp.einsum('bhd,bhtd->bht', n, q) + jnp.sum(s, axis=-1)
    h = num / jnp.maximum(jnp.abs(nq), jnp.exp(-m_t))[..., None]
    m_new = m_t[..., -1]
    w_state = jnp.exp(b[..., -1:] - b + ig - m_new[..., None])
    decay = jnp.exp(b[..., -1] + m - m_new)
    C_new = decay[..., None, None] * C + jnp.einsum('bhs,bhsv,bhsd->bhvd', w_state, v, k)
    n_new = decay[..., None] * n + jnp.einsum('bhs,bhsd->bhd', w_state, k)
    return (C_new, n_new, m_new), h

def mlstm(q, k, v, ig, lf, C0, n0, m0):
    B, H, L, d = q.shape
    Lc = min(L, MLSTM_CHUNK)
    nC = L // Lc

    def to_chunks(a):
        return jnp.moveaxis(a.reshape((B, H, nC, Lc) + a.shape[3:]), 2, 0)

    (C, n, m), hs = lax.scan(_mlstm_chunk_step, (C0, n0, m0),
                             (to_chunks(q), to_chunks(k), to_chunks(v), to_chunks(ig), to_chunks(lf)))
    h = jnp.moveaxis(hs, 0, 2).reshape(B, H, L, d)
    return h, (C, n, m)

def chunk_mlp(u, v, w_s_l, b_s_l, vn_g):
    B, L, _ = v.shape
    Lc = min(L, CHUNK_B)
    nC = L // Lc
    vn = rmsnorm(jax.nn.gelu(v).reshape(B, L, G_B, DG_B), vn_g.reshape(G_B, DG_B))
    w = w_s_l[:, :Lc, :Lc] * jnp.tril(jnp.ones((Lc, Lc), dtype=w_s_l.dtype))
    z = jnp.einsum('gts,bnsgc->bntgc', w, vn.reshape(B, nC, Lc, G_B, DG_B)) + b_s_l[:, :Lc].T[:, :, None]
    out = jax.nn.gelu(u) * z.reshape(B, L, W_B)
    return out, vn.reshape(B, L, W_B)

def parallel_mixer(xn, conv_buf, C0, n0, m0, w_in_l, conv_w_l, conv_b_l, b_i, b_f, hn_g, vn_g, w_s_l, b_s_l, w_out_l):
    B, L, _ = xn.shape
    qk_pre, v_a, o_a, ig, fg, u_b, v_b = jnp.split(xn @ w_in_l, SPLIT_POINTS, axis=-1)
    xp = jnp.concatenate([conv_buf.astype(qk_pre.dtype), qk_pre], axis=1)
    qk = conv_b_l
    for j in range(CONV_W):
        qk = qk + xp[:, j:j + L] * conv_w_l[j]
    qk = jax.nn.silu(qk)
    new_conv = xp[:, L:]
    q, k = jnp.split(qk, 2, axis=-1)

    def heads(a):
        return a.reshape(B, L, H_A, DH_A).transpose(0, 2, 1, 3).astype(jnp.float32)

    ig_h = (ig + b_i).astype(jnp.float32).transpose(0, 2, 1)
    lf_h = jax.nn.log_sigmoid((fg + b_f).astype(jnp.float32)).transpose(0, 2, 1)
    h_a, (C, n, m) = mlstm(heads(q), heads(k) * (DH_A ** -0.5), heads(v_a), ig_h, lf_h,
                           C0.astype(jnp.float32), n0.astype(jnp.float32), m0.astype(jnp.float32))
    h_a = rmsnorm(h_a, hn_g.reshape(H_A, 1, DH_A)).transpose(0, 2, 1, 3).reshape(B, L, W_A)
    h_a = h_a.astype(xn.dtype) * jax.nn.sigmoid(o_a)
    h_b, v_rows = chunk_mlp(u_b, v_b, w_s_l, b_s_l, vn_g)
    y = jnp.concatenate([h_a, h_b], axis=-1) @ w_out_l
    return y, (new_conv, C.astype(C0.dtype), n.astype(n0.dtype), m.astype(m0.dtype), v_rows)

def grouped_ffn(xf, expert_idx, weights, w1_l, w3_l, w2_l):
    T, D = xf.shape
    A = T * TOP_K_IN_GROUP
    e_flat = expert_idx.reshape(A)
    tok = jnp.repeat(jnp.arange(T, dtype=jnp.int32), TOP_K_IN_GROUP)
    w_flat = weights.reshape(A)
    order = jnp.argsort(e_flat)
    e_sorted = e_flat[order]
    counts = jnp.zeros((N_EXPERTS,), jnp.int32).at[e_flat].add(1)
    padded = (counts + MOE_BLOCK - 1) // MOE_BLOCK * MOE_BLOCK
    start = jnp.cumsum(counts) - counts
    pstart = jnp.cumsum(padded) - padded
    dest = pstart[e_sorted] + (jnp.arange(A, dtype=jnp.int32) - start[e_sorted])
    n_blocks = -(-A // MOE_BLOCK) + N_EXPERTS
    n_rows = n_blocks * MOE_BLOCK
    row_tok = jnp.full((n_rows,), T, jnp.int32).at[dest].set(tok[order])
    row_w = jnp.zeros((n_rows,), w_flat.dtype).at[dest].set(w_flat[order])
    block_expert = jnp.minimum(jnp.searchsorted(jnp.cumsum(padded), jnp.arange(n_blocks, dtype=jnp.int32) * MOE_BLOCK, side='right'), N_EXPERTS - 1)
    x_pad = jnp.concatenate([xf, jnp.zeros((1, D), xf.dtype)], axis=0)
    x_blocks = x_pad[row_tok].reshape(n_blocks, MOE_BLOCK, D)

    def expert_block(args):
        xb, e = args
        return (jax.nn.silu(xb @ w1_l[e]) * (xb @ w3_l[e])) @ w2_l[e]

    y = lax.map(expert_block, (x_blocks, block_expert)).reshape(n_rows, D)
    return jax.ops.segment_sum(y * row_w[:, None], row_tok, num_segments=T + 1)[:T]

def hier_moe(x, rg_w, rg_b, re_w, re_b, w1_l, w3_l, w2_l):
    B, L, D = x.shape
    T = B * L
    xf = x.reshape(T, D)
    g_prob = jax.nn.softmax((xf @ rg_w + rg_b).astype(jnp.float32), axis=-1)
    g_sel = jnp.argmax(g_prob, axis=-1)
    g_w = jnp.take_along_axis(g_prob, g_sel[:, None], axis=-1)
    e_logits = (xf @ re_w + re_b).astype(jnp.float32).reshape(T, N_GROUPS, EXPERTS_PER_GROUP)
    e_logits = jnp.take_along_axis(e_logits, g_sel[:, None, None], axis=1)[:, 0]
    top_v, top_i = lax.top_k(e_logits, TOP_K_IN_GROUP)
    weights = g_w * jax.nn.softmax(top_v, axis=-1)
    expert_idx = (g_sel[:, None] * EXPERTS_PER_GROUP + top_i).astype(jnp.int32)
    y = grouped_ffn(xf, expert_idx, weights.astype(x.dtype), w1_l, w3_l, w2_l)
    return y.reshape(B, L, D)

def trunk_layer(x, p, conv_buf, C0, n0, m0, lp):
    (g_mix, w_in_l, conv_w_l, conv_b_l, b_i, b_f, hn_g, vn_g, w_s_l, b_s_l, w_out_l,
     g_ffn, rg_w, rg_b, re_w, re_b, w1_l, w3_l, w2_l, w_ple_l, ple_g, w_pg) = lp
    mix, new_state = parallel_mixer(rmsnorm(x, g_mix), conv_buf, C0, n0, m0, w_in_l, conv_w_l, conv_b_l,
                                    b_i, b_f, hn_g, vn_g, w_s_l, b_s_l, w_out_l)
    h = x + mix
    h = h + hier_moe(rmsnorm(h, g_ffn), rg_w, rg_b, re_w, re_b, w1_l, w3_l, w2_l)
    h = h + jax.nn.sigmoid(h @ w_pg) * rmsnorm(p @ w_ple_l, ple_g)
    return h, new_state

def setup_inputs(seed: int = 0) -> dict:
    key = jax.random.key(seed)
    ks = iter(jax.random.split(key, 48))

    def nrm(shape, scale):
        return scale * jax.random.normal(next(ks), shape, jnp.float32)

    def gain(shape):
        return 1.0 + nrm(shape, 0.05)

    f_bias = jnp.linspace(3.0, 6.0, H_A, dtype=jnp.float32)[None, :] + nrm((DEPTH, H_A), 0.1)
    return {
        'x_prompt': nrm((BATCH, SEQ, D_MODEL), 1.0),
        'x_sample': nrm((DEC_BATCH, DEC_SEQ, D_MODEL), 1.0),
        'state_C': nrm((DEPTH, DEC_BATCH, H_A, DH_A, DH_A), 0.3),
        'state_n': nrm((DEPTH, DEC_BATCH, H_A, DH_A), 0.3),
        'state_m': jax.random.uniform(next(ks), (DEPTH, DEC_BATCH, H_A), jnp.float32, -1.0, 2.0),
        'state_conv': nrm((DEPTH, DEC_BATCH, CONV_W - 1, QK_W), 1.0),
        'p_prompt': nrm((DEPTH, BATCH, SEQ, PLE_DIM), 1.0),
        'p_sample': nrm((DEPTH, DEC_BATCH, DEC_SEQ, PLE_DIM), 1.0),
        'norm_mix_g': gain((DEPTH, D_MODEL)),
        'w_in': nrm((DEPTH, D_MODEL, D_IN), D_MODEL ** -0.5),
        'conv_w': nrm((DEPTH, CONV_W, QK_W), CONV_W ** -0.5),
        'conv_b': nrm((DEPTH, QK_W), 0.02),
        'b_igate': nrm((DEPTH, H_A), 0.1),
        'b_fgate': f_bias,
        'hnorm_g': gain((DEPTH, W_A)),
        'vnorm_g': gain((DEPTH, W_B)),
        'w_s': nrm((DEPTH, G_B, CHUNK_B, CHUNK_B), CHUNK_B ** -0.5),
        'b_s': 1.0 + nrm((DEPTH, G_B, CHUNK_B), 0.1),
        'w_out': nrm((DEPTH, D_MIX, D_MODEL), D_MIX ** -0.5),
        'norm_ffn_g': gain((DEPTH, D_MODEL)),
        'router_g_w': nrm((DEPTH, D_MODEL, N_GROUPS), D_MODEL ** -0.5),
        'router_g_b': nrm((DEPTH, N_GROUPS), 0.01),
        'router_e_w': nrm((DEPTH, D_MODEL, N_EXPERTS), D_MODEL ** -0.5),
        'router_e_b': nrm((DEPTH, N_EXPERTS), 0.01),
        'w1': nrm((DEPTH, N_EXPERTS, D_MODEL, D_FF_EXPERT), D_MODEL ** -0.5),
        'w3': nrm((DEPTH, N_EXPERTS, D_MODEL, D_FF_EXPERT), D_MODEL ** -0.5),
        'w2': nrm((DEPTH, N_EXPERTS, D_FF_EXPERT, D_MODEL), D_FF_EXPERT ** -0.5),
        'w_ple': nrm((DEPTH, PLE_DIM, D_MODEL), PLE_DIM ** -0.5),
        'ple_norm_g': gain((DEPTH, D_MODEL)),
        'w_ple_gate': nrm((DEPTH, D_MODEL, D_MODEL), D_MODEL ** -0.5),
        'final_norm_g': gain((D_MODEL,)),
    }

def reference(x_prompt, x_sample, state_C, state_n, state_m, state_conv, p_prompt, p_sample,
              norm_mix_g, w_in, conv_w, conv_b, b_igate, b_fgate, hnorm_g, vnorm_g, w_s, b_s, w_out,
              norm_ffn_g, router_g_w, router_g_b, router_e_w, router_e_b, w1, w3, w2,
              w_ple, ple_norm_g, w_ple_gate, final_norm_g):
    B = x_prompt.shape[0]
    f32 = jnp.float32
    hp = x_prompt
    hs = x_sample
    Cp, np_, mp, cbp = [], [], [], []
    Cs, ns, ms, cbs, vs = [], [], [], [], []
    for l in range(DEPTH):
        lp = (norm_mix_g[l], w_in[l], conv_w[l], conv_b[l], b_igate[l], b_fgate[l], hnorm_g[l], vnorm_g[l],
              w_s[l], b_s[l], w_out[l], norm_ffn_g[l], router_g_w[l], router_g_b[l], router_e_w[l], router_e_b[l],
              w1[l], w3[l], w2[l], w_ple[l], ple_norm_g[l], w_ple_gate[l])
        hp, (cb_p, C_p, n_p, m_p, _) = trunk_layer(
            hp, p_prompt[l], jnp.zeros((B, CONV_W - 1, QK_W), x_prompt.dtype),
            jnp.zeros((B, H_A, DH_A, DH_A), f32), jnp.zeros((B, H_A, DH_A), f32), jnp.zeros((B, H_A), f32), lp)
        hs, (cb_s, C_s, n_s, m_s, v_s) = trunk_layer(
            hs, p_sample[l], state_conv[l], state_C[l], state_n[l], state_m[l], lp)
        Cp.append(C_p); np_.append(n_p); mp.append(m_p); cbp.append(cb_p)
        Cs.append(C_s); ns.append(n_s); ms.append(m_s); cbs.append(cb_s); vs.append(v_s)
    y_prompt = rmsnorm(hp, final_norm_g)
    y_sample = rmsnorm(hs, final_norm_g)
    return (y_prompt, y_sample,
            jnp.stack(Cp), jnp.stack(np_), jnp.stack(mp), jnp.stack(cbp),
            jnp.stack(Cs), jnp.stack(ns), jnp.stack(ms), jnp.stack(cbs), jnp.stack(vs))


_drawn_inputs = setup_inputs


def setup_inputs(seed=0):
    import zlib

    import numpy as np

    out = dict(_drawn_inputs(seed))
    spreads = {}
    factors = {'router_g_b': 8.0, 'router_e_b': 4.867}
    for name, (base, spread) in spreads.items():
        noise = np.random.default_rng([zlib.crc32(name.encode()), seed]).standard_normal(out[name].shape)
        drawn = base * np.exp(spread * noise) if base else spread * noise
        out[name] = __import__('jax').numpy.asarray(drawn.astype(out[name].dtype))
    for name, factor in factors.items():
        out[name] = (out[name] * factor).astype(out[name].dtype)
    return out
```

```python
from contextlib import ExitStack

import concourse.bass as bass
from concourse import mybir

F32 = mybir.dt.float32
F32R = mybir.dt.float32r
I32 = mybir.dt.int32
ALU = mybir.AluOpType
ACT = mybir.ActivationFunctionType
AX = mybir.AxisListType.X

P = 128
D = 1024
KD = D // P
SEQ = 2048
NT = SEQ // P
NS = 8
NTILE = NT + 1
H = 4
QK = 1024
DIN = 3080
C_V, C_O, C_G, C_U, C_B = 1024, 1536, 2048, 2056, 2568
CW = 4
NG, EPG = 4, 8
NE = NG * EPG
FF = 512
KF = FF // P
CAP = SEQ + P
MAXBLK = NE + (SEQ + NS) * 2 // P
PLE = 256
KP = PLE // P
EPS = 1e-6
BIG = 1e30
GELU_A = 0.044715
GELU_C = 0.7978845608028654
KSCALE = float(P) ** -0.5
TB = NS * H

(S_FABS, S_CONV, S_GIN, S_EXPS, S_QK, S_GSQ, S_NSTATE, S_DIAG, S_VN, S_CSTATE, S_HSQ, S_MIX) = (
    3, 14, 17, 23, 26, 28, 30, 40, 42, 60, 53, 57)


class Steps:

    def __init__(self, eng, sem, tile, per_tile):
        self.eng, self.sem, self.per = eng, sem, per_tile
        self.base = tile * per_tile
        self.n = 0

    def do(self, ins):
        ins.then_inc(self.sem, 1)
        self.n += 1

    def settle(self):
        self.eng.wait_ge(self.sem, self.base + self.n)

    def end(self):
        assert self.n == self.per, (self.sem, self.n)


def program(nc, a, o):
    with ExitStack() as whole:
        def sem(name):
            return whole.enter_context(nc.semaphore(name))

        def dram(name, shape, dt=F32):
            return nc.dram_tensor(name, shape, dt, kind="Internal").ap()

        def keep(name, shape, dt=F32):
            return whole.enter_context(nc.sbuf_tensor(name, shape, dt))

        h_dram = dram("h_dram", (NTILE * P, D))
        hn_dram = dram("hn_dram", (NTILE * P, D))
        list_dram = dram("list_dram", (NE * CAP, 1), I32)
        y_dram = dram("y_dram", ((MAXBLK + 1) * P, D))
        gates_dram = dram("gates_dram", (H, 2, NS))
        kq_dram = dram("kq_dram", (2, TB * P))

        PS = [whole.enter_context(nc.psum_tensor(f"bank{i}", [P, 512], F32)) for i in range(8)]

        ident = keep("ident", [P, P])
        ones = keep("ones", [P, P])
        lead = keep("lead", [P, 2, NTILE])
        place = keep("place", [P, 2, NTILE])
        wtok = keep("wtok", [P, 2, NTILE])
        seen = keep("seen", [P, NE])
        blk = keep("blk", [P, 2, NE], I32)
        yrow = keep("yrow", [P, 2, NTILE], I32)
        rowbase = keep("rowbase", [P, 2, NTILE])
        neghalf = keep("neghalf", [P, 32])
        ecap = keep("ecap", [P, NE])

        const_done = sem("const_done")
        dve_const = sem("dve_const")
        turn = sem("turn")

        def hold(pool, semaphore, value):
            pool.wait_ge(semaphore, value)
            pool.sem_inc(turn, 1)

        with ExitStack() as mix_scope:
            def sb(name, shape, dt=F32):
                return mix_scope.enter_context(nc.sbuf_tensor(name, shape, dt))

            w_in = sb("w_in", [P, KD, DIN])
            w_out = sb("w_out", [P, KD, D])
            gffn_b = sb("gffn_b", [P, D])
            vng_b = sb("vng_b", [P, 512])
            hng_b = sb("hng_b", [P, 512])
            wst = sb("wst", [P, H, P])
            bst = sb("bst", [P, H])
            gmix = sb("gmix", [P, KD])
            cwt = sb("cwt", [P, KD, CW + 1])
            rw = sb("rw", [P, KD, NG + NE])
            rb_b = sb("rb_b", [P, NG + NE])
            gate_b = sb("gate_b", [H, 2])
            tri = sb("tri", [P, P])
            tri_c = sb("tri_c", [P, P])
            sel4 = sb("sel4", [H, H, P])
            rank4 = sb("rank4", [P, NG])
            rank32 = sb("rank32", [P, NE])
            iota_i = sb("iota_i", [P, NE], I32)
            tok = sb("tok", [P, 1], I32)

            x_sb = sb("x_sb", [P, D])
            xr_sb = sb("xr_sb", [P, D])
            junk = sb("junk", [P, D], mybir.dt.bfloat16)
            stat = sb("stat", [P, 64])
            xT = sb("xT", [P, KD, P])
            qkin = sb("qkin", [P, KD, P + CW - 1])
            qkT = sb("qkT", [P, KD, P])
            cv = qkT
            th = sb("th", [P, KD, P])
            rows = sb("rows", [H, 8, P])
            mprev = sb("mprev", [H, 1])
            carry = sb("carry", [H, 1])
            cols = sb("cols", [P, 2 * H])
            vaug = sb("vaug", [P, H, P + 1])
            kw = sb("kw", [P, H, P])
            og = sb("og", [P, 512])
            uv = sb("uv", [P, 2, 512])
            ge = sb("ge", [P, 2, 512])
            gt = th[:, :, :].rearrange("p (a k) n -> p a (k n)", a=2)
            dm = sb("dm", [P, H, P])
            sp = sb("sp", [P, H, P])
            state = sb("state", [P, H, P + 1])
            decay = sb("decay", [P, H])
            hh = dm
            vn = sp
            mix = sb("mix", [P, D])
            mixT = sb("mixT", [P, KD, P])
            h_sb = mix
            hn = sb("hn", [P, D])
            xs = hn
            hnT = mixT
            qs = qkT[:, 0:H, :]
            wsraw = dm
            zero_i = mix[:, 0:NE * CAP // P].bitcast(I32)
            small_in = hn[0:KD, 0:(CW + 2) * P].rearrange("k (j p) -> k j p", p=P)
            bsr = hn[0:H, (CW + 2) * P:(CW + 3) * P]
            lg = sb("lg", [P, NG + NE])
            rt = sb("rt", [P, 6, NE])
            rs = sb("rs", [P, 24])
            idx = sb("idx", [P, 2], I32)
            taken = sb("taken", [P, NE])

            T = [PS[0], PS[1]]
            Q = [PS[2], PS[3]]
            PA, PB, SS, MS = PS[4], PS[5], PS[6], PS[7]
            GATE_I, GATE_F = MS[0:H, 0:P], MS[0:H, P:2 * P]
            COLS = MS[:, 256:256 + 2 * H]
            GATES = MS[:, 272:272 + 2 * H]
            LOG = T[1][:, 0:NG + NE]
            POS = SS[:, 0:NE]

            def heads(bank):
                return bank[:, :].rearrange("p (h n) -> p h n", h=4)

            def pairs(bank):
                return bank[:, 0:2 * (P + 1)].rearrange("p (h n) -> p h n", h=2)

            chunk_steps = sem("chunk_steps")
            route_steps = sem("route_steps")
            pool_steps = sem("pool_steps")
            w_scaled = sem("w_scaled")
            w_scaled_act = sem("w_scaled_act")
            wo_loaded = sem("wo_loaded")
            small_loaded = sem("small_loaded")
            list_zeroed = sem("list_zeroed")
            x_loaded = sem("x_loaded")
            xr_loaded = sem("xr_loaded")
            h_stored = sem("h_stored")
            hn_stored = sem("hn_stored")
            x_sq = sem("x_sq")
            x_rstd = sem("x_rstd")
            xs_ready = sem("xs_ready")
            x_tp = sem("x_tp")
            xT_ready = sem("xT_ready")
            gates_mm = sem("gates_mm")
            gates_in = sem("gates_in")
            gates_tp = sem("gates_tp")
            qk_mm = sem("qk_mm")
            qk_in = sem("qk_in")
            conv_ready = sem("conv_ready")
            qk_tanh = sem("qk_tanh")
            qkT_ready = sem("qkT_ready")
            gate_abs = sem("gate_abs")
            gate_ln = sem("gate_ln")
            rows_ready = sem("rows_ready")
            em_ready = sem("em_ready")
            v_mm = sem("v_mm")
            o_mm = sem("o_mm")
            u_mm = sem("u_mm")
            vb_mm = sem("vb_mm")
            v_in = sem("v_in")
            o_tanh = sem("o_tanh")
            vb_in = sem("vb_in")
            mix_ready = sem("mix_ready")
            mix_tp = sem("mix_tp")
            mixT_ready = sem("mixT_ready")
            y_mm = sem("y_mm")
            h_ready = sem("h_ready")
            h_sq = sem("h_sq")
            h_rstd = sem("h_rstd")
            hn_ready = sem("hn_ready")
            hn_tp = sem("hn_tp")
            hnT_ready = sem("hnT_ready")
            log_mm = sem("log_mm")
            gelu_w = sem("gelu_w")
            gelu_in = sem("gelu_in")
            gelu_tanh = sem("gelu_tanh")
            gelu_ready = sem("gelu_ready")
            mb_mm = sem("mb_mm")
            wib_mm = sem("wib_mm")
            cols_mm = sem("cols_mm")
            s_mm = sem("s_mm")
            k_tp = sem("k_tp")
            dlog_ready = sem("dlog_ready")
            dm_exp = sem("dm_exp")
            dm_ready = sem("dm_ready")
            qs_ready = sem("qs_ready")
            sp_ready = sem("sp_ready")
            kw_ready = sem("kw_ready")
            num_mm = sem("num_mm")
            st_mm = sem("st_mm")
            state_done = sem("state_done")
            gv_sq = sem("gv_sq")
            gv_rstd = sem("gv_rstd")
            vn_ready = sem("vn_ready")
            z_mm = sem("z_mm")
            z_used = sem("z_used")
            hh_ready = sem("hh_ready")
            hh_sq = sem("hh_sq")
            hh_rstd = sem("hh_rstd")
            ha_ready = sem("ha_ready")
            sg_ready = sem("sg_ready")
            g_neg = sem("g_neg")
            e_diff = sem("e_diff")
            e_exp = sem("e_exp")
            oh_ready = sem("oh_ready")
            pos_mm = sem("pos_mm")
            idx_ready = sem("idx_ready")
            scattered = sem("scattered")
            p_steps = sem("p_steps")
            pw_steps = sem("pw_steps")
            prep_tp = sem("prep_tp")
            prep_in = sem("prep_in")
            rank_steps = sem("rank_steps")
            s_load = sem("s_load")
            s_stage = sem("s_stage")
            s_pe = sem("s_pe")
            s_evac = sem("s_evac")
            s_dve = sem("s_dve")
            s_act = sem("s_act")
            s_pool = sem("s_pool")
            s_out = sem("s_out")
            cnt_mm = sem("cnt_mm")
            tail_steps = sem("tail_steps")
            prep_loaded = sem("prep_loaded")
            s_pw = sem("s_pw")
            rstd_x_steps = sem("rstd_x_steps")
            rstd_h_steps = sem("rstd_h_steps")
            tok_steps = sem("tok_steps")

            w_in_loaded = [sem(f"w_in_loaded{g}") for g in range(4)]
            W_IN_PARTS = ((0, 4, 0, C_V), (4, KD, 0, C_V), (0, KD, C_V, C_U), (0, KD, C_U, DIN))
            x_rows = a["x_prompt"].rearrange("b s d -> (b s) d")
            xs_rows = a["x_sample"].rearrange("b s d -> (b s) d")
            scr = w_in[:, :, :].rearrange("p k c -> p (k c)")
            kb = scr[:, 0:4096].rearrange("p (b d) -> p b d", b=TB)
            qb = scr[:, 4096:8192].rearrange("p (b d) -> p b d", b=TB)
            cs = scr[:, 8192:12288].rearrange("p (b d) -> p b d", b=TB)
            tmp = scr[:, 12288:16384].rearrange("p (b d) -> p b d", b=TB)
            thf = th[:, :, :].rearrange("p k n -> p (k n)")
            spf = sp[:, :, :].rearrange("p k n -> p (k n)")
            gef = ge[:, :, :].rearrange("p k n -> p (k n)")
            uvf = uv[:, :, :].rearrange("p k n -> p (k n)")
            s_pr = thf[:, 0:192].rearrange("p (c b) -> p c b", b=NS)
            s_cb = thf[:, 192:448].rearrange("p (k b j) -> p k b j", b=NS, j=CW)
            s_cp = thf[:, 448:704].rearrange("p (k b j) -> p k b j", b=NS, j=CW)
            s_x = thf[:, 704:768].rearrange("p (k b) -> p k b", b=NS)
            s_t = thf[:, 768:832].rearrange("p (k b) -> p k b", b=NS)
            s_qkb = thf[:, 832:896].rearrange("p (w b h) -> p w b h", b=NS, h=H)
            s_vc = thf[:, 896:1024].rearrange("p (w c) -> p w c", c=TB)
            s_dg = gef[0:TB, 5 * P:6 * P].rearrange("p (w c) -> p w c", c=TB)
            s_bc = spf[:, 0:128].rearrange("p (w c) -> p w c", c=TB)
            s_gl = spf[:, 192:384].rearrange("p (w k b) -> p w k b", w=3, b=NS)
            s_m8 = spf[:, 384:448].rearrange("p (k b) -> p k b", b=NS)
            s_col = spf[:, 448:464]
            s_sc = spf[0:TB, 464:488]
            s_g4 = rows[:, 0, 0:2 * NS].rearrange("p (w b) -> p w b", w=2)
            s_st = qkT[0:24, :, :].rearrange("p k n -> p (k n)")
            s_row = gef[0:TB, 0:5 * P].rearrange("p (w d) -> p w d", w=5)
            C_out = kw
            conv_out = uvf[0:CW - 1, :]
            conv_row = xT[0:NS, :, :].rearrange("p k n -> p (k n)")
            vn_rows = vaug[0:NS, 0:4, 0:P]

            with nc.Block() as block:
                @block.sync
                def _(sp_):
                    sp_.dma_start(x_sb[:, :], x_rows[0:P, :]).then_inc(x_loaded, 16)
                    sp_.dma_start(small_in[:, CW + 1, :], a["norm_mix_g"][0].rearrange("(k p) -> k p", p=P)).then_inc(prep_loaded, 16)
                    sp_.dma_start(small_in[:, 0:CW, :], a["conv_w"][0].rearrange("j (k p) -> k j p", p=P)).then_inc(prep_loaded, 16)
                    sp_.dma_start(small_in[:, CW, :], a["conv_b"][0].rearrange("(k p) -> k p", p=P)).then_inc(prep_loaded, 16)
                    sp_.dma_start(bsr, a["b_s"][0]).then_inc(prep_loaded, 16)
                    sp_.dma_start(wsraw[:, :, :], a["w_s"][0].rearrange("g t s -> t g s")).then_inc(prep_loaded, 16)
                    with nc.allow_non_contiguous_dma(reason="eight gate biases"):
                        sp_.dma_start(gate_b[:, 0:1], a["b_igate"].rearrange("l h -> h l")).then_inc(prep_loaded, 16)
                        sp_.dma_start(gate_b[:, 1:2], a["b_fgate"].rearrange("l h -> h l")).then_inc(prep_loaded, 16)
                    sp_.wait_ge(const_done, 1)
                    sp_.dma_start(list_dram.rearrange("(p n) a -> p (n a)", p=P), zero_i).then_inc(list_zeroed, 16)
                    for g, (k0, k1, c0, c1) in enumerate(W_IN_PARTS):
                        for k in range(k0, k1):
                            sp_.dma_start(w_in[:, k, c0:c1], a["w_in"][0, k * P:(k + 1) * P, c0:c1]).then_inc(w_in_loaded[g], 16)
                    sp_.dma_start(gffn_b[:, :], a["norm_ffn_g"][0, :].partition_broadcast(P)).then_inc(small_loaded, 16)
                    sp_.dma_start(vng_b[:, :], a["vnorm_g"][0, :].partition_broadcast(P)).then_inc(small_loaded, 16)
                    sp_.dma_start(hng_b[:, :], a["hnorm_g"][0, :].partition_broadcast(P)).then_inc(small_loaded, 16)
                    sp_.dma_start(rb_b[:, 0:NG], a["router_g_b"][0, :].partition_broadcast(P)).then_inc(small_loaded, 16)
                    sp_.dma_start(rb_b[:, NG:], a["router_e_b"][0, :].partition_broadcast(P)).then_inc(small_loaded, 16)
                    sp_.dma_start(rw[:, :, 0:NG], a["router_g_w"][0].rearrange("(k p) g -> p k g", p=P)).then_inc(small_loaded, 16)
                    sp_.dma_start(rw[:, :, NG:], a["router_e_w"][0].rearrange("(k p) g -> p k g", p=P)).then_inc(small_loaded, 16)
                    sp_.dma_start(w_out[:, :, :], a["w_out"][0].rearrange("(k p) n -> p k n", p=P)).then_inc(wo_loaded, 16)

                    def tile(t, first_, last, prefetch):
                        if prefetch:
                            sp_.wait_ge(xs_ready, t + 1)
                            sp_.dma_start(x_sb[:, :], x_rows[bass.ds((t + 1) * P, P), :]).then_inc(x_loaded, 16)
                        if not first_:
                            if not isinstance(t, int) or t > 1:
                                sp_.wait_ge(h_ready, t - 1)
                            sp_.dma_start(xr_sb[:, :], x_rows[bass.ds((t - 1) * P, P), :]).then_inc(xr_loaded, 16)
                            sp_.wait_ge(h_ready, t)
                            sp_.dma_start(h_dram[bass.ds((t - 1) * P, P), :], h_sb[:, :]).then_inc(h_stored, 16)
                            sp_.wait_ge(hn_ready, t)
                            sp_.dma_start(hn_dram[bass.ds((t - 1) * P, P), :], hn[:, :]).then_inc(hn_stored, 16)

                    tile(0, True, False, True)
                    sp_.dma_start(xr_sb[:, :], x_rows[0:P, :]).then_inc(xr_loaded, 16)
                    sp_.wait_ge(xs_ready, 2)
                    sp_.dma_start(x_sb[:, :], x_rows[2 * P:3 * P, :]).then_inc(x_loaded, 16)
                    sp_.wait_ge(h_ready, 1)
                    sp_.dma_start(h_dram[0:P, :], h_sb[:, :]).then_inc(h_stored, 16)
                    sp_.wait_ge(hn_ready, 1)
                    sp_.dma_start(hn_dram[0:P, :], hn[:, :]).then_inc(hn_stored, 16)
                    with sp_.Fori(2, NT - 1) as t:
                        tile(t, False, False, True)
                    tile(NT - 1, False, False, False)
                    tile(NT, False, True, False)

                    sp_.wait_ge(xs_ready, NT)
                    sp_.dma_start(x_sb[0:NS, :], xs_rows).then_inc(s_load, 16)
                    sp_.wait_ge(mix_ready, NT)
                    sp_.wait_ge(state_done, NT)
                    sp_.dma_start(s_st[:, :], a["state_conv"][0].rearrange("b j c -> (b j) c")).then_inc(s_load, 16)
                    sp_.dma_start(s_row[:, 0, :], a["state_n"][0].rearrange("b h d -> (b h) d")).then_inc(s_load, 16)
                    with nc.allow_non_contiguous_dma(reason="a few scalars per sample and head"):
                        sp_.dma_start(s_sc[:, 0:1], a["state_m"].rearrange("l b h -> (b h) l")).then_inc(s_load, 16)
                        for b in range(NS):
                            sp_.dma_start(s_sc[b * H:(b + 1) * H, 1:2], a["b_igate"].rearrange("l h -> h l")).then_inc(s_load, 16)
                            sp_.dma_start(s_sc[b * H:(b + 1) * H, 2:3], a["b_fgate"].rearrange("l h -> h l")).then_inc(s_load, 16)
                        sp_.dma_start(s_col[:, 0:H], a["w_s"][0, :, 0, 0].partition_broadcast(P)).then_inc(s_load, 16)
                        sp_.dma_start(s_col[:, H:2 * H], a["b_s"][0, :, 0].partition_broadcast(P)).then_inc(s_load, 16)
                        sp_.dma_start(s_col[:, 2 * H:3 * H], a["hnorm_g"][0].rearrange("(h p) -> p h", p=P)).then_inc(s_load, 16)
                        sp_.dma_start(s_col[:, 3 * H:4 * H], a["vnorm_g"][0].rearrange("(h p) -> p h", p=P)).then_inc(s_load, 16)
                    sp_.dma_start(o["conv_s"][0, :, 0:2, :], a["state_conv"][0, :, 1:3, :]).then_inc(s_out, 16)
                    sp_.wait_ge(tail_steps, 2)
                    sp_.dma_start(o["C_p"][0, 0].rearrange("h v d -> v h d"), C_out[:, :, :]).then_inc(s_out, 16)
                    sp_.dma_start(o["n_p"][0, 0], og[0:H, 0:P]).then_inc(s_out, 16)
                    with nc.allow_non_contiguous_dma(reason="four scalars"):
                        sp_.dma_start(o["m_p"][0].rearrange("b h -> h b"), carry[:, :]).then_inc(s_out, 16)
                    sp_.wait_ge(tail_steps, 4)
                    sp_.dma_start(o["conv_p"][0, 0], conv_out).then_inc(s_out, 16)
                    sp_.wait_ge(s_evac, 3)
                    sp_.dma_start(gates_dram, s_g4[:, :, :]).then_inc(s_stage, 16)
                    sp_.wait_ge(s_stage, 16)
                    with nc.allow_non_contiguous_dma(reason="two gates of 32 heads"):
                        for w in range(2):
                            for b in range(NS):
                                sp_.dma_start(s_sc[b * H:(b + 1) * H, 3 + w:4 + w],
                                              gates_dram[:, w, b:b + 1]).then_inc(s_stage, 16)
                    sp_.wait_ge(s_evac, 2)
                    sp_.dma_start(cs, a["state_C"][0].rearrange("b h v d -> v (b h) d")).then_inc(s_load, 16)
                    sp_.wait_ge(s_evac, 6)
                    sp_.dma_start(kq_dram.rearrange("w (b d) -> b w d", b=TB), s_row[:, 1:3, :]).then_inc(s_stage, 16)
                    sp_.wait_ge(s_stage, 16 * 18)
                    sp_.dma_start(scr[:, 0:4096], kq_dram[1, :].partition_broadcast(P)).then_inc(s_stage, 16)
                    sp_.dma_start(scr[:, 4096:8192], kq_dram[0, :].partition_broadcast(P)).then_inc(s_stage, 16)
                    sp_.wait_ge(s_evac, 5)
                    sp_.dma_start(o["conv_s"][0, :, 2, :], conv_row).then_inc(s_out, 16)
                    sp_.wait_ge(s_dve, S_NSTATE)
                    sp_.dma_start(o["n_s"][0].rearrange("b h d -> (b h) d"), s_row[:, 3, :]).then_inc(s_out, 16)
                    with nc.allow_non_contiguous_dma(reason="32 scalars"):
                        sp_.dma_start(o["m_s"].rearrange("l b h -> (b h) l"), s_sc[:, 8:9]).then_inc(s_out, 16)
                    sp_.wait_ge(s_evac, 7)
                    sp_.dma_start(o["v_s"][0].rearrange("b s (h c) -> (b s) h c", h=H), vn_rows).then_inc(s_out, 16)
                    sp_.wait_ge(h_ready, NT)
                    sp_.dma_start(xr_sb[0:NS, :], xs_rows).then_inc(xr_loaded, 16)
                    sp_.wait_ge(s_dve, S_CSTATE)
                    sp_.dma_start(o["C_s"][0].rearrange("b h v d -> v (b h) d"), cs).then_inc(s_out, 16)
                    sp_.wait_ge(h_ready, NT + 1)
                    sp_.dma_start(h_dram[NT * P:NT * P + NS, :], h_sb[0:NS, :]).then_inc(h_stored, 16)
                    sp_.wait_ge(hn_ready, NT + 1)
                    sp_.dma_start(hn_dram[NT * P:NT * P + NS, :], hn[0:NS, :]).then_inc(hn_stored, 16)
                    sp_.wait_ge(h_stored, 16 * NTILE)
                    sp_.wait_ge(hn_stored, 16 * NTILE)
                    sp_.wait_ge(s_out, 16 * 10)


                def hn_transposes_sample(pe):
                    pe.wait_ge(hn_ready, NTILE)
                    for k in range(KD):
                        ins = pe.transpose(T[k // 4][:, (k % 4) * P:(k % 4) * P + NS], hn[0:NS, k * P:(k + 1) * P], ident[0:NS, 0:NS])
                    ins.then_inc(hn_tp, 1)

                @block.tensor
                def _(pe):
                    def mm_k(out, lhs, rhs, n):
                        for k in range(n):
                            ins = pe.matmul(out, lhs(k), rhs(k), start=(k == 0), stop=(k == n - 1))
                        return ins

                    def transposes(src, rows_):
                        for k in range(KD):
                            ins = pe.transpose(T[k // 4][:, (k % 4) * P:(k % 4) * P + rows_],
                                               src[0:rows_, k * P:(k + 1) * P], ident[0:rows_, 0:rows_])
                        return ins

                    def project(t, first_):
                        pe.wait_ge(xs_ready, t + 1)
                        transposes(xs, P).then_inc(x_tp, 1)
                        pe.wait_ge(xT_ready, 2 * t + 2)
                        def gates():
                            mm_k(GATES, lambda k: xT[:, k, :], lambda k: w_in[:, k, C_G:C_U], KD).then_inc(gates_mm, 1)

                        def gate_transposes():
                            pe.wait_ge(gates_in, t + 1)
                            pe.transpose(GATE_I, stat[:, 56:56 + H], ident[:, :])
                            pe.transpose(GATE_F, stat[:, 60:60 + H], ident[:, :]).then_inc(gates_tp, 1)

                        if not first_:
                            gates()
                            pe.wait_ge(hh_ready, t)
                        for half in range(2):
                            for c in range(4 * half, 4 * half + 4):
                                ins = mm_k(Q[half][:, (c % 4) * P:(c % 4 + 1) * P],
                                           lambda k: w_in[:, k, c * P:(c + 1) * P], lambda k: xT[:, k, :], KD)
                            ins.then_inc(qk_mm, 1)
                            if half == 0 and not first_:
                                gate_transposes()
                        if first_:
                            pe.wait_ge(w_scaled, 8)
                            pe.wait_ge(w_scaled_act, 8)
                            gates()
                            gate_transposes()

                    def mix_transposes(u, rows_):
                        pe.wait_ge(mix_ready, u + 1)
                        transposes(mix, rows_).then_inc(mix_tp, 1)

                    def wide(bank, col, done):
                        mm_k(bank[:, :], lambda k: xT[:, k, :], lambda k: w_in[:, k, col:col + 512], KD).then_inc(done, 1)

                    def project_vo(t, first_):
                        if not first_:
                            pe.wait_ge(state_done, t)
                        wide(PA, C_V, v_mm)
                        wide(PB, C_O, o_mm)

                    def project_u(t):
                        pe.wait_ge(v_in, t + 1)
                        wide(PA, C_U, u_mm)

                    def project_vb(t):
                        pe.wait_ge(o_tanh, t + 1)
                        wide(PB, C_B, vb_mm)

                    def out_projection(u, lhs, rows_):
                        for n in range(2):
                            mm_k(Q[n][0:rows_, :], lhs, lambda k: w_out[:, k, n * 512:(n + 1) * 512], KD).then_inc(y_mm, 1)

                    def hn_transposes(u, rows_):
                        pe.wait_ge(hn_ready, u + 1)
                        pe.wait_ge(mixT_ready, 2 * u + 2)
                        transposes(hn, rows_).then_inc(hn_tp, 1)

                    def logits(u, rows_):
                        pe.wait_ge(hnT_ready, 2 * u + 2)
                        mm_k(LOG[0:rows_, :], lambda k: hnT[:, k, 0:rows_], lambda k: rw[:, k, :], KD).then_inc(log_mm, 1)

                    def positions(u, rows_):
                        pe.wait_ge(oh_ready, u + 1)
                        pe.matmul(POS[0:rows_, :], tri[0:rows_, 0:rows_], taken[0:rows_, :], start=True, stop=False)
                        pe.matmul(POS[0:rows_, :], ones[:, 0:rows_], seen[:, :], start=False, stop=True).then_inc(pos_mm, 1)

                    def spread_rows(t):
                        pe.wait_ge(rows_ready, t + 1)
                        for h in range(H):
                            ins = pe.matmul(heads(T[0])[:, h, :], sel4[:, h, :], rows[:, 4, :], start=True, stop=True)
                        ins.then_inc(mb_mm, 1)
                        pe.wait_ge(em_ready, t + 1)
                        for h in range(H):
                            ins = pe.matmul(heads(T[1])[:, h, :], sel4[:, h, :], rows[:, 6, :], start=True, stop=True)
                        ins.then_inc(wib_mm, 1)
                        pe.transpose(COLS[:, 0:H], rows[:, 0, :], ident[0:H, 0:H])
                        pe.transpose(COLS[:, H:2 * H], rows[:, 7, :], ident[0:H, 0:H]).then_inc(cols_mm, 1)

                    def scores(t):
                        pe.wait_ge(qkT_ready, t + 1)
                        for h in range(H):
                            ins = pe.matmul(heads(SS)[:, h, :], qkT[:, H + h, :], qkT[:, h, :], start=True, stop=True)
                        ins.then_inc(s_mm, 1)

                    def k_transposes(t):
                        pe.wait_ge(sp_ready, t + 1)
                        for h in range(H):
                            ins = pe.transpose(heads(SS)[:, h, :], qkT[:, H + h, :], ident[:, :])
                        ins.then_inc(k_tp, 1)

                    def numerators(t):
                        pe.wait_ge(qs_ready, t + 1)
                        for h in range(H):
                            out = pairs(Q[h // 2])[:, h % 2, :]
                            pe.matmul(out, qs[:, h, :], state[:, h, :], start=True, stop=False)
                            ins = pe.matmul(out, sp[:, h, :], vaug[:, h, :], start=False, stop=True)
                        ins.then_inc(num_mm, 1)

                    def state_update(t):
                        pe.wait_ge(kw_ready, t + 1)
                        pe.wait_ge(vb_in, t + 1)
                        for h in range(H):
                            ins = pe.matmul(pairs([PA, PB][h // 2])[:, h % 2, :], kw[:, h, :], vaug[:, h, :], start=True, stop=True)
                        ins.then_inc(st_mm, 1)

                    def chunk_mlp(t, second):
                        pe.wait_ge(vn_ready, t + 1)
                        if not second:
                            pe.wait_ge(idx_ready, t)
                        for g in range(H):
                            ins = pe.matmul(heads(SS)[:, g, :], wst[:, g, :], vn[:, g, :], start=True, stop=True)
                        ins.then_inc(z_mm, 1)

                    def tile(t, first_, second, last):
                        if not last:
                            project(t, first_)
                        if not first_:
                            chunk_mlp(t - 1, second)
                        if not last:
                            project_vo(t, first_)
                        if not first_:
                            mix_transposes(t - 1, P)
                            pe.wait_ge(mixT_ready, 2 * t)
                            if not last:
                                pe.wait_ge(qk_in, 2 * t + 2)
                            out_projection(t - 1, lambda k: mixT[:, k, :], P)
                        if not last:
                            scores(t)
                            spread_rows(t)
                            if first_:
                                pe.wait_ge(const_done, 3 + KD)
                            project_u(t)
                        if not first_:
                            if not last:
                                pe.wait_ge(dlog_ready, t + 1)
                                pe.wait_ge(qs_ready, t + 1)
                            hn_transposes(t - 1, P)
                        if not last:
                            k_transposes(t)
                            project_vb(t)
                        if not first_:
                            logits(t - 1, P)
                        if not last:
                            numerators(t)
                            state_update(t)
                        if not first_:
                            if not last:
                                pe.wait_ge(kw_ready, t + 1)
                            positions(t - 1, P)

                    pe.wait_ge(const_done, 2)
                    pe.wait_ge(prep_loaded, 16 * 7)
                    for j in range(CW + 2):
                        pe.transpose(SS[:, j * KD:(j + 1) * KD], small_in[:, j, :], ident[0:KD, 0:KD])
                    pe.transpose(SS[:, 64:64 + H], bsr, ident[0:H, 0:H]).then_inc(prep_tp, 1)
                    for g in range(H):
                        ins = pe.transpose(heads(PA)[:, g, :], wsraw[:, g, :], ident[:, :])
                    ins.then_inc(prep_tp, 1)
                    pe.wait_ge(prep_in, 4)
                    pe.wait_ge(w_scaled, 4)
                    pe.wait_ge(w_scaled_act, 4)
                    pe.wait_ge(const_done, 3)
                    tile(0, True, False, False)
                    pe.wait_ge(wo_loaded, 16)
                    tile(1, False, True, False)
                    with pe.Fori(2, NT) as t:
                        tile(t, False, False, False)
                    tile(NT, False, False, True)

                    pe.wait_ge(state_done, NT)
                    pe.wait_ge(idx_ready, NT)
                    for h in range(H):
                        pe.transpose(heads(PA)[:, h, :], state[:, h, 0:P], ident[:, :])
                    pe.transpose(SS[0:H, 0:P], state[:, :, P], ident[:, :]).then_inc(s_pe, 1)
                    for k in range(KD):
                        ins = pe.transpose(Q[k // 4][0:CW - 1, (k % 4) * P:(k % 4 + 1) * P], qkin[:, k, 0:CW - 1], ident[:, :])
                    ins.then_inc(s_pe, 1)
                    pe.wait_ge(xs_ready, NT + 1)
                    pe.wait_ge(hnT_ready, 2 * NT)
                    transposes(xs, NS).then_inc(s_pe, 1)
                    pe.wait_ge(s_evac, 1)
                    pe.wait_ge(tail_steps, 4)
                    for c in range(24):
                        col = c * P if c < 16 else c * P + 2 * H
                        mm_k(PB[:, c * NS:(c + 1) * NS], lambda k: w_in[:, k, col:col + P], lambda k: xT[:, k, 0:NS], KD)
                    for g in range(2):
                        ins = mm_k(SS[0:H, g * NS:(g + 1) * NS], lambda k: w_in[:, k, C_G + g * H:C_G + (g + 1) * H],
                                   lambda k: xT[:, k, 0:NS], KD)
                    ins.then_inc(s_pe, 1)
                    pe.wait_ge(s_load, 16 * 24)
                    for k in range(KD):
                        ins = pe.transpose(T[0][:, k * 24:(k + 1) * 24], s_st[:, k * P:(k + 1) * P], ident[0:24, 0:24])
                    ins.then_inc(s_pe, 1)
                    pe.wait_ge(s_evac, 2)
                    for k in range(KD):
                        ins = pe.transpose(Q[k // 4][0:NS, (k % 4) * P:(k % 4 + 1) * P], s_pr[:, k, :], ident[:, :])
                    ins.then_inc(s_pe, 1)
                    pe.wait_ge(s_dve, S_QK)
                    pe.wait_ge(s_evac, 4)
                    for w in range(2):
                        ins = pe.transpose(T[0][0:TB, w * P:(w + 1) * P],
                                           s_qkb[:, w, :, :].rearrange("p b h -> p (b h)"), ident[:, :])
                    ins.then_inc(s_pe, 1)
                    pe.wait_ge(s_dve, S_GSQ)
                    pe.matmul(PA[:, 0:TB], ones[:, :], s_vc[:, 3, :], start=True, stop=True).then_inc(s_pe, 1)
                    pe.wait_ge(s_dve, S_VN)
                    pe.wait_ge(s_evac, 5)
                    for g in range(H):
                        ins = pe.transpose(Q[0][0:NS, g * P:(g + 1) * P], s_gl[:, 2, g, :], ident[:, :])
                    ins.then_inc(s_pe, 1)
                    pe.wait_ge(s_dve, S_DIAG)
                    pe.matmul(SS[:, 0:4 * TB], ones[0:TB, :], s_dg[:, :, :].rearrange("p a b -> p (a b)"),
                              start=True, stop=True).then_inc(s_pe, 1)
                    pe.wait_ge(s_dve, S_HSQ)
                    pe.matmul(PA[:, 64:64 + TB], ones[:, :], s_vc[:, 2, :], start=True, stop=True).then_inc(s_pe, 1)
                    pe.wait_ge(s_dve, S_MIX)
                    pe.wait_ge(s_evac, 8)
                    out_projection(NT, lambda k: s_m8[:, k, :], NS)
                    hn_transposes_sample(pe)
                    logits(NT, NS)
                    positions(NT, NS)
                    pe.wait_ge(idx_ready, NTILE)
                    pe.matmul(POS, ones[:, :], seen[:, :], start=True, stop=True).then_inc(cnt_mm, 1)

                @block.scalar
                def _(act):
                    def copy(out, in_):
                        return act.activation(out, in_, ACT.Copy)

                    def square_x(t):
                        act.wait_ge(x_loaded, 16 * (t + 1))
                        if not isinstance(t, int) or t > 1:
                            act.wait_ge(h_sq, t - 1)
                        elif t == 1:
                            act.wait_ge(x_sq, 1)
                        act.activation(junk[:, :], x_sb[:, :], ACT.Square, accum_out=stat[:, 0:1]).then_inc(x_sq, 1)

                    def squares(buf, at, col, done):
                        for h in range(H):
                            ins = act.activation(junk[:, (at + h) * P:(at + h + 1) * P], buf[:, h, :], ACT.Square, accum_out=stat[:, col + h:col + h + 1])
                        ins.then_inc(done, 1)

                    def tile(t, first_, last, prefetch):
                        if not last:
                            act.wait_ge(x_tp, t + 1)
                            for half in range(2):
                                copy(xT[:, 4 * half:4 * half + 4, :], heads(T[half])).then_inc(xT_ready, 1)
                        if not first_:
                            act.wait_ge(gelu_in, t)
                            act.activation(gt[:, :, :], ge[:, :, :], ACT.Tanh, scale=GELU_C).then_inc(gelu_tanh, 1)
                            act.wait_ge(hh_ready, t)
                            act.wait_ge(x_sq, t if last else t + 1)
                            squares(hh, 4, 24, hh_sq)
                        if not last:
                            act.wait_ge(qk_mm, 2 * t + 1)
                            if not first_:
                                act.wait_ge(conv_ready, t)
                            copy(qkin[:, 0:4, CW - 1:], heads(Q[0])).then_inc(qk_in, 1)
                        if not first_:
                            act.wait_ge(gelu_ready, t)
                            squares(ge[:, 1, :].rearrange("p (h n) -> p h n", h=H), 0, 16, gv_sq)
                        if not last:
                            act.wait_ge(gate_abs, t + 1)
                            act.activation(rows[:, 2, :], rows[:, 2, :], ACT.Exp, scale=-1.0).then_inc(pw_steps, 1)
                            act.wait_ge(qk_mm, 2 * t + 2)
                            copy(qkin[:, 4:8, CW - 1:], heads(Q[1])).then_inc(qk_in, 1)
                            act.wait_ge(pw_steps, t + 1)
                            act.activation(rows[:, 2, :], rows[:, 2, :], ACT.Ln, bias=1.0).then_inc(gate_ln, 1)
                            act.wait_ge(v_mm, t + 1)
                            copy(vaug[:, :, 0:P], heads(PA)).then_inc(v_in, 1)
                            act.wait_ge(conv_ready, t + 1)
                            act.activation(th[:, :, :], cv[:, :, :], ACT.Tanh).then_inc(qk_tanh, 1)
                            act.wait_ge(rows_ready, t + 1)
                            act.activation(rows[:, 6, :], rows[:, 4, :], ACT.Exp, bias=mprev[:, 0:1])
                            act.activation(rows[:, 7, :], rows[:, 5, :], ACT.Exp, scale=-1.0).then_inc(em_ready, 1)
                            act.wait_ge(o_mm, t + 1)
                            if not first_:
                                act.wait_ge(ha_ready, t)
                            act.activation(og[:, :], PB[:, :], ACT.Tanh, scale=0.5).then_inc(o_tanh, 1)
                        if not first_:
                            act.wait_ge(mix_tp, t)
                            for half in range(2):
                                copy(mixT[:, 4 * half:4 * half + 4, :], heads(T[half])).then_inc(mixT_ready, 1)
                            act.wait_ge(h_ready, t)
                            act.wait_ge(gv_sq, t)
                            act.wait_ge(hh_sq, t)
                            act.activation(junk[:, :], h_sb[:, :], ACT.Square, accum_out=stat[:, 8:9]).then_inc(h_sq, 1)
                        if prefetch:
                            square_x(t + 1)
                        if not last:
                            act.wait_ge(dlog_ready, t + 1)
                            act.activation(dm[:, :, :], dm[:, :, :], ACT.Exp).then_inc(dm_exp, 1)
                            act.wait_ge(u_mm, t + 1)
                            copy(uv[:, 0, :], PA[:, :])
                        if not first_:
                            act.wait_ge(hn_tp, t)
                            for half in range(2):
                                copy(hnT[:, 4 * half:4 * half + 4, :], heads(T[half])).then_inc(hnT_ready, 1)
                        if not last:
                            act.wait_ge(vb_mm, t + 1)
                            copy(uv[:, 1, :], PB[:, :]).then_inc(vb_in, 1)
                        if not first_:
                            routing_exps(t - 1, P)

                    def routing_exps(u, r):
                        act.wait_ge(g_neg, u + 1)
                        act.activation(rs[0:r, 4:8], lg[0:r, 0:NG], ACT.Exp, bias=rs[0:r, 0:1], accum_out=rs[0:r, 1:2])
                        act.wait_ge(e_diff, u + 1)
                        act.activation(rs[0:r, 9:10], rs[0:r, 8:9], ACT.Exp).then_inc(e_exp, 1)

                    act.wait_ge(prep_tp, 1)
                    act.activation(cwt[:, :, :], SS[:, 0:KD * (CW + 1)].rearrange("p (j k) -> p k j", k=KD), ACT.Copy, scale=0.5).then_inc(prep_in, 1)
                    copy(gmix[:, :], SS[:, KD * (CW + 1):KD * (CW + 2)]).then_inc(prep_in, 1)
                    copy(bst[:, :], SS[:, 64:64 + H]).then_inc(prep_in, 1)
                    act.wait_ge(prep_tp, 2)
                    copy(wsraw[:, :, :], heads(PA)).then_inc(prep_in, 1)
                    square_x(0)
                    act.wait_ge(prep_in, 4)
                    for g, (k0, k1, c0, c1) in enumerate(W_IN_PARTS[:3]):
                        act.wait_ge(w_in_loaded[g], 16 * (k1 - k0))
                        for k in range(k0, k1, 2):
                            act.activation(w_in[:, k, c0:c1], w_in[:, k, c0:c1], ACT.Copy, scale=gmix[:, k:k + 1]).then_inc(w_scaled_act, 1)
                    tile(0, True, False, True)
                    with act.Fori(1, NT - 1) as t:
                        tile(t, False, False, True)
                    tile(NT - 1, False, False, False)
                    tile(NT, False, True, False)

                    act.wait_ge(s_pe, 1)
                    act.wait_ge(hh_rstd, NT)
                    copy(C_out[:, :, :], heads(PA)).then_inc(tail_steps, 1)
                    act.wait_ge(mix_ready, NT)
                    copy(og[0:H, 0:P], SS[0:H, 0:P]).then_inc(tail_steps, 1)
                    act.wait_ge(s_pe, 2)
                    for half in range(2):
                        copy(conv_out[:, half * 512:(half + 1) * 512], Q[half][0:CW - 1, :]).then_inc(tail_steps, 1)
                    act.wait_ge(s_load, 16 * 24)
                    act.wait_ge(h_sq, NT)
                    act.activation(junk[0:NS, :], x_sb[0:NS, :], ACT.Square, accum_out=stat[0:NS, 0:1]).then_inc(x_sq, 1)
                    act.wait_ge(s_pe, 3)
                    for half in range(2):
                        ins = copy(xT[:, 4 * half:4 * half + 4, 0:NS], heads(T[half])[:, :, 0:NS])
                    ins.then_inc(s_evac, 1)
                    act.wait_ge(s_pe, 4)
                    copy(s_pr[:, :, :], PB[:, 0:24 * NS].rearrange("p (c b) -> p c b", b=NS)).then_inc(s_evac, 1)
                    copy(s_g4[:, :, :], SS[0:H, 0:2 * NS].rearrange("p (w b) -> p w b", w=2)).then_inc(s_evac, 1)
                    act.wait_ge(s_pe, 5)
                    for j in range(CW - 1):
                        ins = copy(s_cb[:, :, :, j], T[0][:, 0:KD * 24].rearrange("p (k b j) -> p k b j", k=KD, j=3)[:, :, :, j])
                    ins.then_inc(s_evac, 1)
                    act.wait_ge(s_pe, 6)
                    copy(conv_row[:, 0:512], Q[0][0:NS, :])
                    copy(conv_row[:, 512:1024], Q[1][0:NS, :]).then_inc(s_evac, 1)
                    act.wait_ge(s_dve, S_FABS)
                    act.activation(s_sc[:, 6:7], s_sc[:, 6:7], ACT.Exp, scale=-1.0).then_inc(s_act, 1)
                    act.wait_ge(s_act, 1)
                    act.activation(s_sc[:, 6:7], s_sc[:, 6:7], ACT.Ln, bias=1.0).then_inc(s_act, 1)
                    act.wait_ge(s_dve, S_CONV)
                    act.activation(s_t[:, :, :], s_x[:, :, :], ACT.Tanh).then_inc(s_act, 1)
                    act.wait_ge(s_pe, 7)
                    copy(s_row[:, 1:3, :], T[0][0:TB, 0:2 * P].rearrange("p (w d) -> p w d", w=2)).then_inc(s_evac, 1)
                    act.wait_ge(s_dve, S_EXPS)
                    act.activation(s_sc[:, 9:12], s_sc[:, 9:12], ACT.Exp).then_inc(s_act, 1)
                    act.wait_ge(s_dve, S_GIN)
                    act.activation(s_gl[:, 1, :, :], s_gl[:, 1, :, :], ACT.Tanh, scale=GELU_C)
                    act.activation(s_vc[:, 0, :].rearrange("p (h b) -> p h b", h=H), s_pr[:, 12:16, :], ACT.Tanh, scale=0.5).then_inc(s_act, 1)
                    act.wait_ge(s_pe, 8)
                    copy(s_vc[:, 3, :], PA[:, 0:TB]).then_inc(s_pw, 1)
                    act.wait_ge(s_pe, 9)
                    copy(vn_rows, heads(Q[0])[0:NS, :, :]).then_inc(s_evac, 1)
                    act.wait_ge(s_pe, 10)
                    copy(s_bc[:, :, :], SS[:, 0:4 * TB].rearrange("p (a b) -> p a b", a=4)).then_inc(s_evac, 1)
                    act.wait_ge(s_pe, 11)
                    copy(s_vc[:, 2, :], PA[:, 64:64 + TB]).then_inc(s_pw, 1)
                    act.wait_ge(h_ready, NTILE)
                    act.wait_ge(x_sq, NTILE)
                    act.activation(junk[0:NS, :], h_sb[0:NS, :], ACT.Square, accum_out=stat[0:NS, 8:9]).then_inc(h_sq, 1)
                    act.wait_ge(hn_tp, NTILE)
                    for half in range(2):
                        copy(hnT[:, 4 * half:4 * half + 4, 0:NS], heads(T[half])[:, :, 0:NS]).then_inc(hnT_ready, 1)
                    routing_exps(NT, NS)

                @block.vector
                def _(dve):
                    TT, TS, STT = dve.tensor_tensor, dve.tensor_scalar, dve.scalar_tensor_tensor

                    def norm_x(t, r=P):
                        dve.wait_ge(x_rstd, t + 1)
                        if not isinstance(t, int) or t > 0:
                            dve.wait_ge(x_tp, t)
                        if not isinstance(t, int) or t > 1:
                            dve.wait_ge(hn_stored, 16 * (t - 1))
                            dve.wait_ge(hn_tp, t - 1)
                        TS(xs[0:r, :], x_sb[0:r, :], stat[0:r, 1:2], None, ALU.mult).then_inc(xs_ready, 1)

                    def gates_1(t):
                        st = Steps(dve, chunk_steps, t, 56)
                        dve.wait_ge(gates_mm, t + 1)
                        dve.tensor_copy(stat[:, 56:64], GATES).then_inc(gates_in, 1)
                        return st

                    def gates_2(t, st):
                        dve.wait_ge(gates_tp, t + 1)
                        if not isinstance(t, int) or t > 0:
                            dve.wait_ge(em_ready, t)
                            dve.wait_ge(cols_mm, t)
                        st.do(TS(rows[:, 1, :], GATE_F, gate_b[:, 1:2], None, ALU.add))
                        st.do(TS(rows[:, 0, :], GATE_I, gate_b[:, 0:1], None, ALU.add))
                        st.settle()
                        STT(rows[:, 2, :], rows[:, 1, :], -1.0, rows[:, 1, :], ALU.mult, ALU.max).then_inc(gate_abs, 1)

                    def gates_3(t, st):
                        dve.wait_ge(gate_ln, t + 1)
                        st.do(STT(rows[:, 2, :], rows[:, 1, :], 0.0, rows[:, 2, :], ALU.min, ALU.subtract))
                        st.settle()
                        st.do(dve.tensor_tensor_scan(rows[:, 1, :], ones[0:H, :], rows[:, 2, :], 0.0, ALU.mult, ALU.add))
                        st.settle()
                        st.do(TT(rows[:, 0, :], rows[:, 0, :], rows[:, 1, :], ALU.subtract))
                        st.settle()
                        st.do(dve.tensor_tensor_scan(rows[:, 3, :], rows[:, 0, :], rows[:, 0, :], carry[:, 0:1], ALU.max, ALU.max))
                        st.settle()
                        st.do(dve.tensor_copy(mprev[:, :], carry[:, :]))
                        st.do(TS(rows[:, 4, :], rows[:, 3, :], -1.0, None, ALU.mult))
                        st.do(TT(rows[:, 5, :], rows[:, 3, :], rows[:, 1, :], ALU.add))
                        st.settle()
                        dve.tensor_copy(carry[:, :], rows[:, 5, P - 1:P]).then_inc(rows_ready, 1)

                    def conv(t, st):
                        for j in range(CW):
                            for k in range(KD):
                                if j == 0 and k % 4 == 0:
                                    dve.wait_ge(qk_in, 2 * t + k // 4 + 1)
                                src = qkin[:, k, j:j + P]
                                if j == 0:
                                    st.do(TS(cv[:, k, :], src, cwt[:, k, 0:1], cwt[:, k, CW:CW + 1], ALU.mult, ALU.add))
                                else:
                                    if k == 0:
                                        st.settle()
                                    st.do(STT(cv[:, k, :], src, cwt[:, k, j:j + 1], cv[:, k, :], ALU.mult, ALU.add))
                        st.settle()
                        st.do(dve.tensor_copy(stat[:, 32:56].rearrange("p (k j) -> p k j", j=3), qkin[:, :, P:P + 3]))
                        st.settle()
                        dve.tensor_copy(qkin[:, :, 0:3], stat[:, 32:56].rearrange("p (k j) -> p k j", j=3)).then_inc(conv_ready, 1)

                    def silu_qk(t):
                        dve.wait_ge(qk_tanh, t + 1)
                        if not isinstance(t, int) or t > 0:
                            dve.wait_ge(k_tp, t)
                        STT(qkT[:, :, :], th[:, :, :], 1.0, cv[:, :, :], ALU.add, ALU.mult).then_inc(qkT_ready, 1)

                    def residual(u, r):
                        dve.wait_ge(xr_loaded, 16 * (u + 1))
                        if not isinstance(u, int) or u > 0:
                            dve.wait_ge(h_stored, 16 * u)
                        for n in range(2):
                            dve.wait_ge(y_mm, 2 * u + n + 1)
                            ins = TT(h_sb[0:r, n * 512:(n + 1) * 512], Q[n][0:r, :], xr_sb[0:r, n * 512:(n + 1) * 512], ALU.add)
                        ins.then_inc(h_ready, 1)

                    def norm_h(u, r):
                        dve.wait_ge(h_rstd, u + 1)
                        if not isinstance(u, int) or u > 0:
                            dve.wait_ge(hn_stored, 16 * u)
                            dve.wait_ge(hn_tp, u)
                        if not isinstance(u, int) or u < NT - 1:
                            dve.wait_ge(x_tp, u + 2)
                        STT(hn[0:r, :], h_sb[0:r, :], stat[0:r, 9:10], gffn_b[0:r, :], ALU.mult, ALU.mult).then_inc(hn_ready, 1)

                    def out_gate(t):
                        dve.wait_ge(o_tanh, t + 1)
                        STT(og[:, :], og[:, :], 1.0, hng_b[:, :], ALU.add, ALU.mult).then_inc(sg_ready, 1)

                    def gelu_inner(t):
                        dve.wait_ge(gelu_w, t + 1)
                        TT(ge[:, :, :], ge[:, :, :], uv[:, :, :], ALU.mult).then_inc(gelu_in, 1)

                    def gelu_outer(t):
                        dve.wait_ge(gelu_tanh, t + 1)
                        STT(ge[:, :, :], gt[:, :, :], 1.0, uv[:, :, :], ALU.add, ALU.mult).then_inc(gelu_ready, 1)

                    def decay_logs(t, st):
                        dve.wait_ge(cols_mm, t + 1)
                        if not isinstance(t, int) or t > 0:
                            dve.wait_ge(sp_ready, t)
                        st.do(dve.tensor_copy(cols[:, :], COLS))
                        st.settle()
                        dve.wait_ge(mb_mm, t + 1)
                        for h in range(H):
                            ins = TS(dm[:, h, :], heads(T[0])[:, h, :], cols[:, h:h + 1], 0.0, ALU.add, ALU.min)
                            if h < H - 1:
                                st.do(ins)
                        ins.then_inc(dlog_ready, 1)
                        dve.wait_ge(wib_mm, t + 1)
                        dve.wait_ge(s_mm, t + 1)
                        if not isinstance(t, int) or t > 0:
                            dve.wait_ge(state_done, t)
                        st.do(dve.tensor_copy(decay[:, :], heads(T[1])[:, :, P - 1]))
                        TT(qs, qkT[:, 0:H, :], heads(T[1]), ALU.mult).then_inc(qs_ready, 1)

                    def route_1(u, r):
                        st = Steps(dve, route_steps, u, 28)
                        dve.wait_ge(log_mm, u + 1)
                        if not isinstance(u, int) or u > 0:
                            dve.wait_ge(idx_ready, u)
                        R = lambda ap: ap[0:r]
                        st.do(TT(lg[0:r, :], LOG[0:r, :], rb_b[0:r, :], ALU.add))
                        st.settle()
                        g, e = lg[0:r, 0:NG], lg[0:r, NG:]
                        st.do(dve.tensor_reduce(rs[0:r, 2:3], g, AX, ALU.max))
                        st.settle()
                        TS(rs[0:r, 0:1], rs[0:r, 2:3], -1.0, None, ALU.mult).then_inc(g_neg, 1)
                        st.do(STT(rt[0:r, 0, 0:NG], g, rs[0:r, 2:3], rank4[0:r, :], ALU.is_equal, ALU.mult))
                        st.settle()
                        st.do(dve.tensor_reduce(rs[0:r, 3:4], rt[0:r, 0, 0:NG], AX, ALU.max))
                        st.settle()
                        st.do(TS(rt[0:r, 0, 0:NG], rt[0:r, 0, 0:NG], rs[0:r, 3:4], BIG, ALU.is_equal, ALU.mult))
                        st.settle()
                        st.do(TS(rt[0:r, 0, 0:NG], rt[0:r, 0, 0:NG], -BIG, None, ALU.add))
                        st.settle()
                        e8 = lambda ap: ap.rearrange("p (g e) -> p g e", g=NG)
                        st.do(TT(e8(rt[0:r, 1, :]), e8(e), rt[0:r, 0, 0:NG].unsqueeze(2).to_broadcast([r, NG, EPG]), ALU.add))
                        st.settle()
                        for n in range(2):
                            top, head = rs[0:r, 10 + n:11 + n], rs[0:r, 12 + n:13 + n]
                            logit = rt[0:r, 1 + n, :]
                            onehot = (rt[0:r, 4, :], rt[0:r, 5, :])[n]
                            st.do(dve.tensor_reduce(top, logit, AX, ALU.max))
                            st.settle()
                            st.do(STT(rt[0:r, 3, :], logit, top, rank32[0:r, :], ALU.is_equal, ALU.mult))
                            st.settle()
                            st.do(dve.tensor_reduce(head, rt[0:r, 3, :], AX, ALU.max))
                            st.settle()
                            st.do(TS(onehot, rt[0:r, 3, :], head, None, ALU.is_equal))
                            st.settle()
                            if n == 0:
                                st.do(STT(rt[0:r, 2, :], onehot, -BIG, logit, ALU.mult, ALU.add))
                                st.settle()
                        TT(rs[0:r, 8:9], rs[0:r, 11:12], rs[0:r, 10:11], ALU.subtract).then_inc(e_diff, 1)
                        st.do(dve.tensor_copy(lead[0:r, :, bass.ds(u, 1)].rearrange("p w a -> p (w a)"), rs[0:r, 12:14]))
                        TT(taken[0:r, :], rt[0:r, 4, :], rt[0:r, 5, :], ALU.add).then_inc(oh_ready, 1)
                        dve.wait_ge(e_exp, u + 1)
                        st.do(dve.reciprocal(rs[0:r, 14:15], rs[0:r, 1:2]))
                        st.do(TS(rs[0:r, 15:16], rs[0:r, 9:10], 1.0, None, ALU.add))
                        st.settle()
                        st.do(dve.reciprocal(rs[0:r, 16:17], rs[0:r, 15:16]))
                        st.settle()
                        return st

                    def route_2(u, r, st):
                        st.do(TT(rs[0:r, 17:18], rs[0:r, 16:17], rs[0:r, 14:15], ALU.mult))
                        st.settle()
                        st.do(TT(rs[0:r, 18:19], rs[0:r, 17:18], rs[0:r, 9:10], ALU.mult))
                        st.settle()
                        st.do(dve.tensor_copy(wtok[0:r, :, bass.ds(u, 1)].rearrange("p w a -> p (w a)"), rs[0:r, 17:19]))
                        dve.wait_ge(pos_mm, u + 1)
                        st.do(TT(rt[0:r, 3, :], POS[0:r, :], ecap[0:r, :], ALU.add))
                        st.settle()
                        for n in range(2):
                            st.do(dve.tensor_tensor_reduce(rt[0:r, 1 + n, :], rt[0:r, 4 + n, :], rt[0:r, 3, :], 1.0, 0.0,
                                                           ALU.mult, ALU.add, rs[0:r, 20 + n:21 + n]))
                        st.settle()
                        if not isinstance(u, int) or u > 0:
                            dve.wait_ge(scattered, 32 * u)
                        st.do(dve.tensor_copy(place[0:r, :, bass.ds(u, 1)].rearrange("p w a -> p (w a)"), rs[0:r, 20:22]))
                        st.do(TT(seen[0:r, :], seen[0:r, :], taken[0:r, :], ALU.add))
                        st.settle()
                        dve.tensor_copy(idx[0:r, :], rs[0:r, 20:22]).then_inc(idx_ready, 1)
                        st.end()

                    def weigh(t):
                        dve.wait_ge(s_mm, t + 1)
                        dve.wait_ge(dm_ready, t + 1)
                        TT(sp[:, :, :], heads(SS), dm[:, :, :], ALU.mult).then_inc(sp_ready, 1)
                        dve.wait_ge(k_tp, t + 1)
                        if not isinstance(t, int) or t > 0:
                            dve.wait_ge(st_mm, t)
                        TT(kw[:, :, :], heads(SS), dm[:, :, P - 1:P].to_broadcast([P, H, P]), ALU.mult).then_inc(kw_ready, 1)

                    def norm_v(t):
                        dve.wait_ge(gv_rstd, t + 1)
                        dve.wait_ge(num_mm, t + 1)
                        gv = ge[:, 1, :].rearrange("p (h n) -> p h n", h=H)
                        if not isinstance(t, int) or t > 0:
                            dve.wait_ge(z_mm, t)
                        for g in range(H):
                            ins = STT(vn[:, g, :], gv[:, g, :], stat[:, 20 + g:21 + g], vng_b[:, g * P:(g + 1) * P], ALU.mult, ALU.mult)
                        ins.then_inc(vn_ready, 1)

                    def divide(t, st):
                        dve.wait_ge(num_mm, t + 1)
                        for n in range(2):
                            st.do(TT(stat[:, 2 + 2 * n:4 + 2 * n], pairs(Q[n])[:, :, P], cols[:, H + 2 * n:H + 2 * n + 2], ALU.max))
                        st.settle()
                        for n in range(2):
                            st.do(STT(stat[:, 2 + 2 * n:4 + 2 * n], pairs(Q[n])[:, :, P], -1.0, stat[:, 2 + 2 * n:4 + 2 * n], ALU.mult, ALU.max))
                        st.settle()
                        st.do(dve.reciprocal(stat[:, 12:16], stat[:, 2:6]))
                        st.settle()
                        for n in range(2):
                            ins = TT(hh[:, 2 * n:2 * n + 2, :], pairs(Q[n])[:, :, 0:P],
                                     stat[:, 12 + 2 * n:14 + 2 * n].unsqueeze(2).to_broadcast([P, 2, P]), ALU.mult)
                            if n == 0:
                                st.do(ins)
                        ins.then_inc(hh_ready, 1)

                    def update(t, st):
                        dve.wait_ge(st_mm, t + 1)
                        for h in range(H):
                            ins = STT(state[:, h, :], state[:, h, :], decay[:, h:h + 1], pairs([PA, PB][h // 2])[:, h % 2, :], ALU.mult, ALU.add)
                            if h < H - 1:
                                st.do(ins)
                        ins.then_inc(state_done, 1)

                    def gated_heads(t):
                        dve.wait_ge(hh_rstd, t + 1)
                        dve.wait_ge(sg_ready, t + 1)
                        if not isinstance(t, int) or t > 0:
                            dve.wait_ge(mix_tp, t)
                            dve.wait_ge(h_stored, 16 * t)
                        for h in range(H):
                            ins = STT(mix[:, h * P:(h + 1) * P], hh[:, h, :], stat[:, 28 + h:29 + h], og[:, h * P:(h + 1) * P], ALU.mult, ALU.mult)
                        ins.then_inc(ha_ready, 1)

                    def mlp_out(t):
                        dve.wait_ge(z_mm, t + 1)
                        dve.wait_ge(ha_ready, t + 1)
                        TT(hh[:, :, :], heads(SS), bst[:, :].unsqueeze(2).to_broadcast([P, H, P]), ALU.add).then_inc(z_used, 1)
                        dve.wait_ge(z_used, t + 1)
                        STT(mix[:, 512:], ge[:, 0, :], 0.5, hh[:, :, :].rearrange("p h n -> p (h n)"), ALU.mult, ALU.mult).then_inc(mix_ready, 1)

                    def tile(t, first_, last, prefetch):
                        if not last:
                            st = gates_1(t)
                        if not first_:
                            gelu_outer(t - 1)
                            gated_heads(t - 1)
                            norm_v(t - 1)
                        if not last:
                            gates_2(t, st)
                        if not first_:
                            mlp_out(t - 1)
                        if not last:
                            conv(t, st)
                            gates_3(t, st)
                            silu_qk(t)
                            out_gate(t)
                        if not first_:
                            residual(t - 1, P)
                            norm_h(t - 1, P)
                        if not last:
                            decay_logs(t, st)
                            weigh(t)
                        if prefetch:
                            norm_x(t + 1)
                        if not first_:
                            rst = route_1(t - 1, P)
                        if not last:
                            divide(t, st)
                            gelu_inner(t)
                            update(t, st)
                            st.end()
                        if not first_:
                            route_2(t - 1, P, rst)

                    for ap, v in ((vaug[:, :, P:], 1.0), (state[:, :, :], 0.0), (carry[:, :], 0.0), (qkin[:, :, :], 0.0),
                                  (seen[:, :], 0.0), (lead[:, :, :], 0.0), (place[:, :, :], 0.0),
                                  (wtok[:, :, :], 0.0)):
                        dve.memset(ap, v).then_inc(dve_const, 1)
                    dve.wait_ge(prep_loaded, 16 * 7)
                    dve.wait_ge(dve_const, 8)
                    norm_x(0)
                    dve.wait_ge(prep_in, 4)
                    dve.wait_ge(const_done, 3)
                    for g, (k0, k1, c0, c1) in enumerate(W_IN_PARTS[:3]):
                        dve.wait_ge(w_in_loaded[g], 16 * (k1 - k0))
                        for k in range(k0 + 1, k1, 2):
                            TS(w_in[:, k, c0:c1], w_in[:, k, c0:c1], gmix[:, k:k + 1], None, ALU.mult).then_inc(w_scaled, 1)
                    dve.wait_ge(small_loaded, 16 * 7)
                    TS(hng_b[:, :], hng_b[:, :], 0.5, None, ALU.mult).then_inc(dve_const, 1)
                    dve.wait_ge(dve_const, 9)
                    tile(0, True, False, True)
                    tile(1, False, False, True)
                    with dve.Fori(2, NT - 1) as t:
                        tile(t, False, False, True)
                    tile(NT - 1, False, False, False)
                    tile(NT, False, True, False)

                    n = [0]
                    marks = {}

                    def do(ins, mark=None):
                        ins.then_inc(s_dve, 1)
                        n[0] += 1
                        if mark:
                            assert n[0] == mark, (n[0], mark)

                    def settle():
                        dve.wait_ge(s_dve, n[0])

                    norm_x(NT, NS)
                    dve.wait_ge(s_stage, 16 * 17)
                    dve.wait_ge(s_load, 16 * 24)
                    sc = lambda c, w=1: s_sc[:, c:c + w]
                    do(TT(sc(5), sc(4), sc(2), ALU.add))
                    do(TT(sc(7), sc(3), sc(1), ALU.add))
                    settle()
                    do(STT(sc(6), sc(5), -1.0, sc(5), ALU.mult, ALU.max), S_FABS)
                    dve.wait_ge(s_evac, 4)
                    do(dve.tensor_copy(s_cb[:, :, :, 3], s_pr[:, 0:KD, :]))
                    settle()
                    for k in range(KD):
                        do(TT(s_cp[:, k, :, :], s_cb[:, k, :, :], cwt[:, k, 0:CW].unsqueeze(1).to_broadcast([P, NS, CW]), ALU.mult))
                    settle()
                    do(dve.tensor_reduce(s_x[:, :, :], s_cp[:, :, :, :], AX, ALU.add))
                    settle()
                    do(TT(s_x[:, :, :], s_x[:, :, :], cwt[:, :, CW:CW + 1].to_broadcast([P, KD, NS]), ALU.add), S_CONV)
                    ux = s_pr[:, 16:24, :]
                    do(TT(s_gl[:, 0, :, :], ux, ux, ALU.mult))
                    settle()
                    do(TS(s_gl[:, 0, :, :], s_gl[:, 0, :, :], GELU_A, 1.0, ALU.mult, ALU.add))
                    settle()
                    do(TT(s_gl[:, 1, :, :], s_gl[:, 0, :, :], ux, ALU.mult), S_GIN)
                    dve.wait_ge(s_act, 3)
                    do(STT(sc(6), sc(5), 0.0, sc(6), ALU.min, ALU.subtract))
                    settle()
                    do(TT(sc(6), sc(6), sc(0), ALU.add))
                    settle()
                    do(TT(sc(8), sc(6), sc(7), ALU.max))
                    settle()
                    do(TT(sc(9), sc(6), sc(8), ALU.subtract))
                    do(TT(sc(10), sc(7), sc(8), ALU.subtract))
                    do(TS(sc(11), sc(8), -1.0, None, ALU.mult), S_EXPS)
                    for w in range(2):
                        out = s_qkb[:, w, :, :].rearrange("p b h -> p h b")
                        do(STT(out, s_t[:, 4 * w:4 * w + 4, :], 1.0, s_x[:, 4 * w:4 * w + 4, :], ALU.add, ALU.mult))
                    settle()
                    do(TS(s_qkb[:, 1, :, :], s_qkb[:, 1, :, :], KSCALE, None, ALU.mult), S_QK)
                    dve.wait_ge(s_act, 5)
                    do(STT(s_gl[:, 0, :, :], s_gl[:, 1, :, :], 1.0, ux, ALU.add, ALU.mult))
                    settle()
                    hb = lambda ap: ap.rearrange("p (h b) -> p h b", h=H)
                    gv = s_gl[:, 0, 4:8, :]
                    do(TT(hb(s_vc[:, 3, :]), gv, gv, ALU.mult), S_GSQ)
                    dve.wait_ge(s_evac, 6)
                    do(TS(s_row[:, 4, :], s_row[:, 2, :], sc(10), None, ALU.mult))
                    settle()
                    do(STT(s_row[:, 3, :], s_row[:, 0, :], sc(9), s_row[:, 4, :], ALU.mult, ALU.add), S_NSTATE)
                    settle()
                    do(dve.tensor_tensor_reduce(s_row[:, 4, :], s_row[:, 3, :], s_row[:, 1, :], 1.0, 0.0, ALU.mult, ALU.add, sc(12)))
                    settle()
                    do(dve.tensor_tensor_reduce(s_row[:, 4, :], s_row[:, 1, :], s_row[:, 2, :], 1.0, 0.0, ALU.mult, ALU.add, sc(15)))
                    settle()
                    do(TT(sc(16), sc(15), sc(10), ALU.mult))
                    do(TT(sc(13), sc(12), sc(11), ALU.max))
                    settle()
                    do(STT(sc(13), sc(12), -1.0, sc(13), ALU.mult, ALU.max))
                    settle()
                    do(dve.reciprocal(sc(14), sc(13)))
                    settle()
                    for i, c in enumerate((9, 10, 14, 16)):
                        do(TS(s_dg[:, i, :], ident[0:TB, 0:TB], sc(c), None, ALU.mult), S_DIAG if i == 3 else None)
                    dve.wait_ge(s_pool, 1)
                    do(TT(s_gl[:, 2, 0:4, :], gv, hb(s_vc[:, 3, :]), ALU.mult))
                    settle()
                    do(TT(s_gl[:, 2, 0:4, :], s_gl[:, 2, 0:4, :], s_col[:, 3 * H:4 * H].unsqueeze(2).to_broadcast([P, H, NS]), ALU.mult), S_VN)
                    settle()
                    do(TT(s_gl[:, 2, 4:8, :], s_gl[:, 2, 0:4, :], s_col[:, 0:H].unsqueeze(2).to_broadcast([P, H, NS]), ALU.mult))
                    settle()
                    do(TT(s_gl[:, 2, 4:8, :], s_gl[:, 2, 4:8, :], s_col[:, H:2 * H].unsqueeze(2).to_broadcast([P, H, NS]), ALU.add))
                    settle()
                    do(STT(s_m8[:, 4:8, :], s_gl[:, 0, 0:4, :], 0.5, s_gl[:, 2, 4:8, :], ALU.mult, ALU.mult))
                    dve.wait_ge(s_evac, 8)
                    bh = lambda ap: ap.rearrange("p (b h) -> p h b", h=H)
                    do(TT(bh(s_vc[:, 3, :]), bh(s_bc[:, 1, :]), s_pr[:, 8:12, :], ALU.mult))
                    do(TT(bh(s_vc[:, 2, :]), bh(s_bc[:, 3, :]), s_pr[:, 8:12, :], ALU.mult))
                    dve.wait_ge(s_stage, 16 * 20)
                    dve.wait_ge(s_load, 16 * 25)
                    wide = lambda ap: ap.unsqueeze(2).to_broadcast([P, TB, P])
                    do(TT(tmp, cs, qb, ALU.mult))
                    settle()
                    do(dve.tensor_reduce(s_vc[:, 1, :], tmp, AX, ALU.add))
                    settle()
                    do(TT(s_vc[:, 1, :], s_vc[:, 1, :], s_bc[:, 0, :], ALU.mult))
                    settle()
                    do(TT(s_vc[:, 1, :], s_vc[:, 1, :], s_vc[:, 2, :], ALU.add))
                    settle()
                    do(TT(s_vc[:, 1, :], s_vc[:, 1, :], s_bc[:, 2, :], ALU.mult))
                    settle()
                    do(TT(s_vc[:, 2, :], s_vc[:, 1, :], s_vc[:, 1, :], ALU.mult), S_HSQ)
                    dve.wait_ge(s_pool, 2)
                    do(TT(s_vc[:, 1, :], s_vc[:, 1, :], s_vc[:, 2, :], ALU.mult))
                    do(TS(s_vc[:, 0, :], s_vc[:, 0, :], 1.0, 0.5, ALU.add, ALU.mult))
                    settle()
                    do(TT(hb(s_vc[:, 0, :]), hb(s_vc[:, 0, :]), s_col[:, 2 * H:3 * H].unsqueeze(2).to_broadcast([P, H, NS]), ALU.mult))
                    settle()
                    do(TT(s_m8[:, 0:4, :], bh(s_vc[:, 1, :]), hb(s_vc[:, 0, :]), ALU.mult), S_MIX)
                    do(TT(tmp, kb, wide(s_vc[:, 3, :]), ALU.mult))
                    do(TT(cs, cs, wide(s_bc[:, 0, :]), ALU.mult))
                    settle()
                    do(TT(cs, cs, tmp, ALU.add), S_CSTATE)
                    residual(NT, NS)
                    norm_h(NT, NS)
                    route_2(NT, NS, route_1(NT, NS))
                    dve.wait_ge(cnt_mm, 1)
                    tl = lambda k: dve.wait_ge(rank_steps, k)
                    TS(blk[:, 0, :], POS, float(P - 1), None, ALU.add).then_inc(rank_steps, 1)
                    tl(1)
                    TS(blk[:, 1, :], blk[:, 0, :], 7, None, ALU.arith_shift_right).then_inc(rank_steps, 1)
                    tl(2)
                    TS(rt[:, 0, :], blk[:, 1, :], 1.0, None, ALU.max).then_inc(rank_steps, 1)
                    tl(3)
                    dve.tensor_tensor_scan(rt[:, 1, :], ones[:, 0:NE], rt[:, 0, :], 0.0, ALU.mult, ALU.add).then_inc(rank_steps, 1)
                    tl(4)
                    TT(rt[:, 2, :], rt[:, 1, :], rt[:, 0, :], ALU.subtract).then_inc(rank_steps, 1)
                    tl(5)
                    dve.tensor_copy(blk[:, 0, :], rt[:, 2, :]).then_inc(rank_steps, 1)
                    dve.tensor_copy(blk[:, 1, :], rt[:, 1, :]).then_inc(rank_steps, 1)
                    STT(rt[:, 3, :], rt[:, 2, :], float(P), ecap[:, :], ALU.mult, ALU.subtract).then_inc(rank_steps, 1)
                    tl(8)
                    k0 = 8
                    hot = scr[:, 0:NTILE * NE].rearrange("p (t e) -> p t e", e=NE)
                    dve.wait_ge(s_out, 16 * 10)
                    for w in range(2):
                        TT(hot, lead[:, w, :].unsqueeze(2).to_broadcast([P, NTILE, NE]),
                           rank32[:, :].unsqueeze(1).to_broadcast([P, NTILE, NE]), ALU.is_equal).then_inc(rank_steps, 1)
                        tl(k0 + 1)
                        TT(hot, hot, rt[:, 3, :].unsqueeze(1).to_broadcast([P, NTILE, NE]), ALU.mult).then_inc(rank_steps, 1)
                        tl(k0 + 2)
                        dve.tensor_reduce(rowbase[:, w, :], hot, AX, ALU.add).then_inc(rank_steps, 1)
                        k0 += 3
                        tl(k0)
                    TT(yrow[:, :, :], rowbase[:, :, :], place[:, :, :], ALU.add).then_inc(rank_steps, 1)
                    tl(15)

                @block.gpsimd
                def _(pool):
                    pool.memset(ident[:, :], 0.0).then_inc(p_steps, 1)
                    pool.memset(zero_i, 0).then_inc(const_done, 1)
                    pool.memset(ones[:, :], 1.0).then_inc(p_steps, 1)
                    pool.memset(tri_c[:, :], KSCALE).then_inc(p_steps, 1)
                    pool.memset(neghalf[:, :], -0.5).then_inc(p_steps, 1)
                    pool.memset(sel4[:, :, :], 1.0).then_inc(p_steps, 1)
                    pool.iota(iota_i[:, :], pattern=[[-1, NE]], base=NE, channel_multiplier=0).then_inc(p_steps, 1)
                    pool.iota(tok[:, :], pattern=[[0, 1]], base=0, channel_multiplier=1).then_inc(p_steps, 1)
                    pool.wait_ge(p_steps, 7)
                    pool.affine_select(out=ident[:, :], in_=ident[:, :], compare_op=ALU.not_equal, fill=1.0, base=0,
                                       pattern=[[-1, P]], channel_multiplier=1).then_inc(const_done, 1)
                    pool.affine_select(out=tri[:, :], in_=ones[:, :], compare_op=ALU.is_gt, fill=0.0, base=0,
                                       pattern=[[1, P]], channel_multiplier=-1).then_inc(p_steps, 1)
                    pool.affine_select(out=tri_c[:, :], in_=tri_c[:, :], compare_op=ALU.is_ge, fill=0.0, base=0,
                                       pattern=[[1, P]], channel_multiplier=-1).then_inc(p_steps, 1)
                    pool.affine_select(out=sel4[:, :, :], in_=sel4[:, :, :], compare_op=ALU.is_equal, fill=0.0, base=0,
                                       pattern=[[1, H], [0, P]], channel_multiplier=-1).then_inc(p_steps, 1)
                    pool.tensor_copy(rank32[:, :], iota_i[:, :]).then_inc(p_steps, 1)
                    pool.tensor_scalar(ecap[:, :], iota_i[:, :], float(-CAP), float(NE * CAP), ALU.mult, ALU.add).then_inc(p_steps, 1)
                    pool.tensor_scalar(rank4[:, :], iota_i[:, NE - NG:], 1.0, None, ALU.mult).then_inc(p_steps, 1)
                    def rstd(rows_, src, dst, width, n, wait, count, done, steps, base, post=1.0):
                        hold(pool, wait, count)
                        pool.tensor_scalar(stat[0:rows_, dst:dst + width], stat[0:rows_, src:src + width], 1.0 / n, EPS,
                                           ALU.mult, ALU.add).then_inc(steps, 1)
                        hold(pool, steps, base + 1)
                        ins = pool.tensor_tensor(stat[0:rows_, dst:dst + width], stat[0:rows_, dst:dst + width],
                                                 neghalf[0:rows_, 0:width], ALU.pow)
                        if post == 1.0:
                            ins.then_inc(done, 1)
                        else:
                            ins.then_inc(steps, 1)
                            hold(pool, steps, base + 2)
                            pool.tensor_scalar(stat[0:rows_, dst:dst + width], stat[0:rows_, dst:dst + width], post, None,
                                               ALU.mult).then_inc(done, 1)

                    def rstd_x(t, r=P):
                        rstd(r, 0, 1, 1, D, x_sq, t + 1, x_rstd, rstd_x_steps, t)

                    def rstd_h(u, r=P):
                        rstd(r, 8, 9, 1, D, h_sq, u + 1, h_rstd, rstd_h_steps, u)

                    def scatter(u, r=P):
                        hold(pool, idx_ready, u + 1)
                        if not isinstance(u, int) or u > 0:
                            hold(pool, tok_steps, u)
                        for w in range(2):
                            pool.indirect_dma_start(out=list_dram, out_offset=bass.IndirectOffsetOnAxis(ap=idx[0:r, w:w + 1], axis=0),
                                                    in_=tok[0:r, :], in_offset=None).then_inc(scattered, 16)
                        hold(pool, scattered, 32 * (u + 1))
                        pool.tensor_scalar(tok[:, :], tok[:, :], float(P), None, ALU.add).then_inc(tok_steps, 1)

                    def tile(t, first_, last, prefetch):
                        if not first_:
                            rstd(P, 24, 28, H, P, hh_sq, t, hh_rstd, pool_steps, 4 * t - 3)
                            rstd(P, 16, 20, H, 4 * P, gv_sq, t, gv_rstd, pool_steps, 4 * t - 2, post=0.5)
                            rstd_h(t - 1)
                        if prefetch:
                            rstd_x(t + 1)
                        if not last:
                            hold(pool, dm_exp, t + 1)
                            pool.tensor_tensor(dm[:, :, :], dm[:, :, :], tri_c[:, :].unsqueeze(1).to_broadcast([P, H, P]), ALU.mult).then_inc(dm_ready, 1)
                            hold(pool, vb_in, t + 1)
                            if not first_:
                                hold(pool, mix_ready, t)
                            pool.tensor_tensor(ge[:, :, :], uv[:, :, :], uv[:, :, :], ALU.mult).then_inc(pool_steps, 1)
                            hold(pool, pool_steps, 4 * t + 1)
                            pool.tensor_scalar(ge[:, :, :], ge[:, :, :], GELU_A, 1.0, ALU.mult, ALU.add).then_inc(gelu_w, 1)
                        if not first_:
                            scatter(t - 1)

                    pool.wait_ge(p_steps, 13)
                    rstd_x(0)
                    pool.wait_ge(prep_in, 4)
                    pool.wait_ge(list_zeroed, 16)
                    pool.affine_select(out=wst[:, :, :], in_=wsraw[:, :, :], compare_op=ALU.is_ge, fill=0.0, base=0,
                                       pattern=[[0, H], [1, P]], channel_multiplier=-1).then_inc(const_done, 1)

                    for k in range(KD):
                        pool.wait_ge(w_in_loaded[3], 16 * KD)
                        pool.tensor_scalar(w_in[:, k, C_U:DIN], w_in[:, k, C_U:DIN], gmix[:, k:k + 1], None, ALU.mult).then_inc(const_done, 1)
                    tile(0, True, False, True)
                    with pool.Fori(1, NT - 1) as t:
                        tile(t, False, False, True)
                    tile(NT - 1, False, False, False)
                    tile(NT, False, True, False)

                    rstd_x(NT, NS)

                    def rstd_sample(slot, n, scale, base):
                        pool.wait_ge(s_pw, slot + 1)
                        v = s_vc[:, 3 - slot, :]
                        pool.tensor_scalar(v, v, 1.0 / n, EPS, ALU.mult, ALU.add).then_inc(p_steps, 1)
                        hold(pool, p_steps, 13 + base + 1)
                        pool.tensor_tensor(v, v, neghalf[:, 0:TB], ALU.pow).then_inc(p_steps, 1)
                        hold(pool, p_steps, 13 + base + 2)
                        pool.tensor_scalar(v, v, scale, None, ALU.mult).then_inc(s_pool, 1)
                    rstd_sample(0, 4 * P, 0.5, 0)
                    rstd_sample(1, P, 1.0, 2)
                    rstd_h(NT, NS)
                    scatter(NT, NS)

        with ExitStack() as late:
            def sb(name, shape, dt=F32):
                return late.enter_context(nc.sbuf_tensor(name, shape, dt))

            w_pg = sb("w_pg", [P, KD, D])
            w_ple = sb("w_ple", [P, KP, D])
            pleg_b = sb("pleg_b", [P, D])
            fing_b = sb("fing_b", [P, D])
            with ExitStack() as expert_scope:
                def eb(name, shape, dt=F32):
                    return expert_scope.enter_context(nc.sbuf_tensor(name, shape, dt))

                w13 = [[eb(f"w{m}_{b}", [P, KD, FF]) for m in (1, 3)] for b in range(2)]
                w2s = [eb(f"w2_{b}", [P, KF, D]) for b in range(2)]
                entry = eb("entry", [P, 1], I32)
                rows_in = eb("rows_in", [P, D])
                xTe = eb("xTe", [P, KD, P])
                tanh_h = eb("tanh_h", [P, FF])
                up = eb("up", [P, FF])
                hid = eb("hid", [P, FF])
                hidT = eb("hidT", [P, KF, P])
                y_sb = eb("y_sb", [P, D])
                T, H1, H3, AT, Y = PS[0:2], PS[2], PS[3], [PS[4], PS[7]], PS[5:7]
                quarter = lambda bank: bank[:, :].rearrange("p (k n) -> p k n", k=4)

                w_sem = [[sem(f"expert_w{m}_{b}") for m in (1, 3, 2)] for b in range(2)]
                (entry_loaded, rows_loaded, xe_tp, xTe_ready, h1_mm, h3_mm, tanh_done, up_done, hid_ready, hid_tp,
                 hidT_ready, y0_mm, y1_mm, y_in, y_stored, late_loaded, spare_filled) = [sem(n) for n in (
                     "entry_loaded rows_loaded xe_tp xTe_ready h1_mm h3_mm tanh_done up_done hid_ready hid_tp "
                     "hidT_ready y0_mm y1_mm y_in y_stored late_loaded spare_filled").split()]

                def span(eng, e):
                    lo = eng.value_load(blk[0:1, 0, bass.ds(e, 1)], min_val=0, max_val=MAXBLK)
                    hi = eng.value_load(blk[0:1, 1, bass.ds(e, 1)], min_val=1, max_val=MAXBLK)
                    return lo, hi

                def all_blocks(eng, body):
                    with eng.Fori(0, NE // 2) as pair:
                        for b in range(2):
                            lo, hi = span(eng, pair * 2 + b)
                            with eng.Fori(lo, hi) as i:
                                body(i, pair, b, lo)

                with nc.Block() as block:
                    @block.sync
                    def _(sp_):
                        def load(e, b, which=(0, 1, 2)):
                            for m in which:
                                dst, src = ((w13[b][0], "w1"), (w13[b][1], "w3"), (w2s[b], "w2"))[m]
                                sp_.dma_start(dst[:, :, :], a[src][0, bass.ds(e, 1), :, :].rearrange(
                                    "a (k p) n -> p (a k) n", p=P)).then_inc(w_sem[b][m], 16)
                        load(0, 0, (0,))
                        sp_.wait_ge(rows_loaded, 16)
                        load(0, 0, (1,))
                        sp_.wait_ge(rows_loaded, 32)
                        load(0, 0, (2,))
                        load(1, 1)
                        def next_pair(pair):
                            for b in range(2):
                                _, hi = span(sp_, pair * 2 + b - 2)
                                sp_.wait_ge(y1_mm, hi)
                                load(pair * 2 + b, b)

                        next_pair(1)
                        for dst, src in ((w_pg[:, :, :], a["w_ple_gate"][0].rearrange("(k p) n -> p k n", p=P)),
                                         (w_ple[:, :, :], a["w_ple"][0].rearrange("(k p) n -> p k n", p=P)),
                                         (pleg_b[:, :], a["ple_norm_g"][0, :].partition_broadcast(P)),
                                         (fing_b[:, :], a["final_norm_g"].partition_broadcast(P))):
                            sp_.dma_start(dst, src).then_inc(late_loaded, 16)
                        next_pair(2)
                        _, total = span(sp_, NE - 1)
                        with sp_.Fori(total, MAXBLK + 1) as i:
                            sp_.dma_start(y_dram[bass.ds(i * P, P), :], hn_dram[0:P, :]).then_inc(spare_filled, 16)
                        with sp_.Fori(0, total) as i:
                            sp_.sem_inc(spare_filled, 16)
                        with sp_.Fori(3, NE // 2) as pair:
                            next_pair(pair)
                        sp_.wait_ge(spare_filled, (MAXBLK + 1) * 16)

                    @block.gpsimd
                    def _(pool):
                        def gather(i, at):
                            at = at if isinstance(at, int) else nc.s_assert_within(at, 0, NE * CAP - P)
                            pool.dma_start(entry[:, :], list_dram[bass.ds(at, P), :]).then_inc(entry_loaded, 16)
                            hold(pool, entry_loaded, 16 * i + 16)
                            hold(pool, xe_tp, i + 1)
                            pool.indirect_dma_start(out=rows_in[:, :], out_offset=None, in_=hn_dram[0:NT * P + NS, :],
                                                    in_offset=bass.IndirectOffsetOnAxis(ap=entry[:, 0:1], axis=0)
                                                    ).then_inc(rows_loaded, 16)
                            hold(pool, rows_loaded, 16 * i + 16)

                        all_blocks(pool, lambda i, pair, b, lo: gather(i, (pair * 2 + b) * CAP + (i - lo) * P))
                        _, total = span(pool, NE - 1)
                        gather(total, 0)

                    @block.tensor
                    def _(pe):
                        def transposes(i):
                            pe.wait_ge(rows_loaded, 16 * i + 16)
                            for k in range(KD):
                                ins = pe.transpose(T[k // 4][:, (k % 4) * P:(k % 4 + 1) * P], rows_in[:, k * P:(k + 1) * P], ident[:, :])
                            ins.then_inc(xe_tp, 1)

                        def blockwork(i, pair, b, lo):
                            pe.wait_ge(xTe_ready, 2 * i + 2)
                            for m, (bank, done) in enumerate(((H1, h1_mm), (H3, h3_mm))):
                                pe.wait_ge(w_sem[b][m], 16 * pair + 16)
                                for k in range(KD):
                                    ins = pe.matmul(bank[:, :], xTe[:, k, :], w13[b][m][:, k, :], start=(k == 0), stop=(k == KD - 1))
                                ins.then_inc(done, 1)
                            transposes(i + 1)
                            pe.wait_ge(hid_ready, i + 1)
                            for k in range(KF):
                                ins = pe.transpose(quarter(AT[k // 2])[:, k % 2, :], hid[:, k * P:(k + 1) * P], ident[:, :])
                            ins.then_inc(hid_tp, 1)
                            pe.wait_ge(hidT_ready, 2 * i + 2)
                            pe.wait_ge(w_sem[b][2], 16 * pair + 16)
                            pe.wait_ge(y_in, 2 * i + 2)
                            for n, done in enumerate((y0_mm, y1_mm)):
                                for k in range(KF):
                                    ins = pe.matmul(Y[n][:, :], hidT[:, k, :], w2s[b][:, k, n * 512:(n + 1) * 512],
                                                    start=(k == 0), stop=(k == KF - 1))
                                ins.then_inc(done, 1)

                        pe.sem_inc(xe_tp, 1)
                        transposes(0)
                        all_blocks(pe, blockwork)

                    @block.scalar
                    def _(act):
                        def xT_half(i):
                            act.wait_ge(xe_tp, i + 2)
                            act.activation(xTe[:, 0:4, :], quarter(T[0]), ACT.Copy).then_inc(xTe_ready, 1)

                        def blockwork(i, pair, b, lo):
                            act.wait_ge(h1_mm, i + 1)
                            act.activation(tanh_h[:, :], H1[:, :], ACT.Tanh, scale=0.5).then_inc(tanh_done, 1)
                            xT_half(i + 1)
                            act.wait_ge(hid_tp, i + 1)
                            act.activation(hidT[:, 0:2, :], quarter(AT[0])[:, 0:2, :], ACT.Copy).then_inc(hidT_ready, 1)
                            act.wait_ge(y0_mm, i + 1)
                            act.wait_ge(y_stored, 16 * i + 16)
                            act.activation(y_sb[:, 0:512], Y[0][:, :], ACT.Copy).then_inc(y_in, 1)
                            act.wait_ge(y_in, 2 * i + 4)
                            act.dma_start(y_dram[bass.ds(i * P, P), :], y_sb[:, :]).then_inc(y_stored, 16)

                        act.sem_inc(y_in, 2)
                        act.sem_inc(y_stored, 16)
                        xT_half(0)
                        all_blocks(act, blockwork)
                        _, total = span(act, NE - 1)
                        act.wait_ge(y_stored, total * 16 + 16)
                        act.sem_inc(turn, 1)

                    @block.vector
                    def _(dve):
                        def xT_half(i):
                            dve.wait_ge(xe_tp, i + 2)
                            dve.tensor_copy(xTe[:, 4:8, :], quarter(T[1])).then_inc(xTe_ready, 1)

                        def blockwork(i, pair, b, lo):
                            dve.wait_ge(tanh_done, i + 1)
                            dve.scalar_tensor_tensor(up[:, :], tanh_h[:, :], 1.0, H1[:, :], ALU.add, ALU.mult).then_inc(up_done, 1)
                            dve.wait_ge(up_done, i + 1)
                            dve.wait_ge(h3_mm, i + 1)
                            dve.scalar_tensor_tensor(hid[:, :], up[:, :], 0.5, H3[:, :], ALU.mult, ALU.mult).then_inc(hid_ready, 1)
                            xT_half(i + 1)
                            dve.wait_ge(hid_tp, i + 1)
                            dve.tensor_copy(hidT[:, 2:4, :], quarter(AT[1])[:, 0:2, :]).then_inc(hidT_ready, 1)
                            dve.wait_ge(y1_mm, i + 1)
                            dve.wait_ge(y_stored, 16 * i + 16)
                            dve.tensor_copy(y_sb[:, 512:], Y[1][:, :]).then_inc(y_in, 1)

                        xT_half(0)
                        all_blocks(dve, blockwork)

            h_in = [sb(f"h_in{b}", [P, D]) for b in range(2)]
            y1 = [sb(f"y1_{b}", [P, D]) for b in range(2)]
            y2 = [sb(f"y2_{b}", [P, D]) for b in range(2)]
            p_in = [sb(f"p_in{b}", [P, PLE]) for b in range(2)]
            yi = [sb(f"yi{b}", [P, 2], I32) for b in range(2)]
            W_IN_SHARE = KD
            pg_hi = sb("pg_hi", [P, KD, D], F32R)
            pg_lo = sb("pg_lo", [P, KD, D], F32R)
            hT_hi = [sb(f"hT_hi{b}", [P, KD, P], F32R) for b in range(2)]
            hT_lo = [sb(f"hT_lo{b}", [P, KD, P], F32R) for b in range(2)]
            hs = sb("hs", [P, 4 * D])
            h2 = [hs[:, b * D:(b + 1) * D] for b in range(2)]
            h3 = hs[:, 2 * D:3 * D]
            outb = hs[:, 3 * D:4 * D]
            hx = sb("hx", [P, 4 * D])
            tg = hx[:, 0:D]
            emb = hx[:, 2 * D:3 * D]
            junk3 = hx[:, 3 * D:4 * D]
            hz = sb("hz", [P, 544])
            pT = [hz[:, b * PLE:(b + 1) * PLE].rearrange("p (k n) -> p k n", k=KP) for b in range(2)]
            st3 = hz[:, 512:544]
            T, PT, L, G = PS[0:2], PS[2], PS[3:5], PS[5:7]
            (yi_ready, h2_part, h2_ready, tp3, hT_hi_ready, hT_lo_ready, pT_ready, ple_mm, gate_mm, ple_sq, gate_tanh,
             ple_rstd, em1, em2, h3_ready, h3_sq, h3_rstd, out_ready, out_stored, pl_steps, p3_steps) = [sem(n) for n in (
                "yi_ready h2_part h2_ready tp3 hT_hi_ready hT_lo_ready pT_ready ple_mm gate_mm ple_sq gate_tanh "
                "ple_rstd em1 em2 h3_ready h3_sq h3_rstd out_ready out_stored pl_steps p3_steps").split()]
            hp_sem = [sem(f"hp_loaded{b}") for b in range(2)]
            yg_sem = [sem(f"y_gathered{b}") for b in range(2)]

            def half(ap, n, r=P):
                return ap[0:r, n * 512:(n + 1) * 512]

            def tiles(tile):
                def loop(eng):
                    with eng.Fori(0, NT // 2 - 1) as pair:
                        for b in range(2):
                            tile(pair * 2 + b, pair, b, P, P, P)
                    tile(NT - 2, NT // 2 - 1, 0, P, P, NS)
                    tile(NT - 1, NT // 2 - 1, 1, P, NS, 0)
                    tile(NT, NT // 2, 0, NS, 0, 0)
                return loop

            with nc.Block() as block:
                p_rows = a["p_prompt"][0].rearrange("b s d -> (b s) d")
                y_out = o["y_p"].rearrange("b s d -> (b s) d")

                @block.sync
                def _(sp_):
                    def load(t, b, r):
                        sp_.dma_start(h_in[b][0:r, :], h_dram[bass.ds(t * P, r), :]).then_inc(hp_sem[b], 16)
                        src = p_rows[bass.ds(t * P, P), :] if r == P else a["p_sample"][0].rearrange("b s d -> (b s) d")
                        sp_.dma_start(p_in[b][0:r, :], src).then_inc(hp_sem[b], 16)

                    def tile(t, turn, b, r, r1, r2):
                        if r2:
                            sp_.wait_ge(h2_ready, t + 1)
                            sp_.wait_ge(tp3, t + 1)
                            load(t + 2, b, r2)
                        sp_.wait_ge(out_ready, t + 1)
                        dst = y_out[bass.ds(t * P, P), :] if r == P else o["y_s"].rearrange("b s d -> (b s) d")
                        sp_.dma_start(dst, outb[0:r, :]).then_inc(out_stored, 16)

                    load(0, 0, P)
                    load(1, 1, P)
                    tiles(tile)(sp_)
                    sp_.wait_ge(out_stored, 16 * NTILE)

                @block.gpsimd
                def _(pool):
                    def gather(t, b, r):
                        pool.tensor_copy(yi[b][0:r, :], yrow[0:r, :, bass.ds(t, 1)].rearrange("p w a -> p (w a)")).then_inc(yi_ready, 1)
                        hold(pool, yi_ready, t + 1)
                        for w, dst in enumerate((y1[b], y2[b])):
                            pool.indirect_dma_start(out=dst[0:r, :], out_offset=None, in_=y_dram,
                                                    in_offset=bass.IndirectOffsetOnAxis(ap=yi[b][0:r, w:w + 1], axis=0)
                                                    ).then_inc(yg_sem[b], 16)

                    def tile(t, turn, b, r, r1, r2):
                        if r2:
                            hold(pool, h2_ready, t + 1)
                            gather(t + 2, b, r2)
                        hold(pool, ple_sq, 2 * t + 2)
                        pool.tensor_tensor(st3[0:r, 2:3], st3[0:r, 0:1], st3[0:r, 1:2], ALU.add).then_inc(pl_steps, 1)
                        hold(pool, pl_steps, 3 * t + 1)
                        pool.tensor_scalar(st3[0:r, 2:3], st3[0:r, 2:3], 1.0 / D, EPS, ALU.mult, ALU.add).then_inc(pl_steps, 1)
                        hold(pool, pl_steps, 3 * t + 2)
                        pool.tensor_tensor(st3[0:r, 2:3], st3[0:r, 2:3], neghalf[0:r, 0:1], ALU.pow).then_inc(pl_steps, 1)
                        hold(pool, pl_steps, 3 * t + 3)
                        pool.tensor_scalar(st3[0:r, 3:4], st3[0:r, 2:3], 0.5, None, ALU.mult).then_inc(ple_rstd, 1)
                        hold(pool, h3_sq, t + 1)
                        pool.tensor_scalar(st3[0:r, 5:6], st3[0:r, 4:5], 1.0 / D, EPS, ALU.mult, ALU.add).then_inc(p3_steps, 1)
                        hold(pool, p3_steps, t + 1)
                        pool.tensor_tensor(st3[0:r, 6:7], st3[0:r, 5:6], neghalf[0:r, 0:1], ALU.pow).then_inc(h3_rstd, 1)

                    gather(0, 0, P)
                    gather(1, 1, P)
                    tiles(tile)(pool)

                @block.tensor
                def _(pe):
                    def transposes(t, b, r):
                        pe.wait_ge(h2_ready, t + 1)
                        for k in range(KD):
                            pe.transpose(T[k // 4][:, (k % 4) * P:(k % 4) * P + r], h2[b][0:r, k * P:(k + 1) * P], ident[0:r, 0:r])
                        for k in range(KP):
                            ins = pe.transpose(PT[:, k * P:k * P + r], p_in[b][0:r, k * P:(k + 1) * P], ident[0:r, 0:r])
                        ins.then_inc(tp3, 1)

                    def tile(t, turn, b, r, r1, r2):
                        pe.wait_ge(pT_ready, t + 1)
                        for n in range(2):
                            pe.wait_ge(em1, 2 * t + 1 + n)
                            for k in range(KP):
                                ins = pe.matmul(L[n][0:r, :], pT[b][:, k, 0:r], half(w_ple[:, k, :], n), start=(k == 0), stop=(k == KP - 1))
                        ins.then_inc(ple_mm, 1)
                        pe.wait_ge(hT_lo_ready, 2 * t + 2)
                        pe.wait_ge(w_scaled, W_IN_SHARE + KD)
                        for n in range(2):
                            for k in range(KD):
                                for p, (x, w) in enumerate(((hT_hi, pg_hi), (hT_hi, pg_lo), (hT_lo, pg_hi))):
                                    ins = pe.matmul(G[n][:, :], x[b][:, k, :], half(w[:, k, :], n), start=(k == 0 and p == 0),
                                                    stop=(k == KD - 1 and p == 2))
                            ins.then_inc(gate_mm, 1)
                            if n == 0 and r1:
                                transposes(t + 1, 1 - b, r1)

                    transposes(0, 0, P)
                    pe.wait_ge(late_loaded, 64)
                    tiles(tile)(pe)

                @block.scalar
                def _(act):
                    def hT_half(t, b, r):
                        quarter = lambda bank: bank[:, :].rearrange("p (k n) -> p k n", k=4)[:, :, 0:r]
                        act.wait_ge(tp3, t + 1)
                        act.activation(pT[b][:, :, 0:r], quarter(PT)[:, 0:KP, :], ACT.Copy).then_inc(pT_ready, 1)
                        for n in range(2):
                            act.activation(hT_hi[b][:, 4 * n:4 * n + 4, 0:r], quarter(T[n]), ACT.Copy).then_inc(hT_hi_ready, 1)

                    def tile(t, turn, b, r, r1, r2):
                        act.wait_ge(ple_mm, t + 1)
                        if not isinstance(t, int) or t > 0:
                            act.wait_ge(h3_sq, t)
                        act.activation(half(junk3, 0, r), L[0][0:r, :], ACT.Square, accum_out=st3[0:r, 0:1]).then_inc(ple_sq, 1)
                        act.activation(half(junk3, 1, r), L[1][0:r, :], ACT.Square, accum_out=st3[0:r, 1:2]).then_inc(ple_sq, 1)
                        for n in range(2):
                            act.wait_ge(gate_mm, 2 * t + n + 1)
                            act.activation(half(tg, n, r), G[n][0:r, :], ACT.Tanh, scale=0.5).then_inc(gate_tanh, 1)
                            if n == 0 and r1:
                                hT_half(t + 1, 1 - b, r1)
                        act.wait_ge(h3_ready, t + 1)
                        act.wait_ge(ple_sq, 2 * t + 2)
                        act.activation(junk3[0:r, :], h3[0:r, :], ACT.Square, accum_out=st3[0:r, 4:5]).then_inc(h3_sq, 1)

                    act.wait_ge(late_loaded, 64)
                    for k in range(KD):
                        act.activation(pg_hi[:, k, :], w_pg[:, k, :], ACT.Copy).then_inc(w_scaled_act, 1)
                    hT_half(0, 0, P)
                    tiles(tile)(act)

                @block.vector
                def _(dve):
                    STT = dve.scalar_tensor_tensor

                    def combine(t, turn, b, r):
                        dve.wait_ge(hp_sem[b], 32 * turn + 32)
                        dve.wait_ge(yg_sem[b], 32 * turn + 32)
                        w = lambda n: wtok[0:r, n, bass.ds(t, 1)]
                        STT(h2[b][0:r, :], y1[b][0:r, :], w(0), h_in[b][0:r, :], ALU.mult, ALU.add).then_inc(h2_part, 1)
                        dve.wait_ge(h2_part, t + 1)
                        STT(h2[b][0:r, :], y2[b][0:r, :], w(1), h2[b][0:r, :], ALU.mult, ALU.add).then_inc(h2_ready, 1)

                    def hT_half(t, b, r):
                        quarter = lambda bank: bank[:, :].rearrange("p (k n) -> p k n", k=4)[:, :, 0:r]
                        for n in range(2):
                            dve.wait_ge(hT_hi_ready, 2 * t + n + 1)
                            dve.tensor_tensor(hT_lo[b][:, 4 * n:4 * n + 4, 0:r], quarter(T[n]), hT_hi[b][:, 4 * n:4 * n + 4, 0:r].bitcast(F32),
                                              ALU.subtract).then_inc(hT_lo_ready, 1)

                    def tile(t, turn, b, r, r1, r2):
                        for n in range(2):
                            dve.wait_ge(gate_tanh, 2 * t + n + 1)
                            STT(half(emb, n, r), half(tg, n, r), 1.0, L[n][0:r, :], ALU.add, ALU.mult).then_inc(em1, 1)
                            if n == 0 and r1:
                                hT_half(t + 1, 1 - b, r1)
                        dve.wait_ge(em1, 2 * t + 4)
                        dve.wait_ge(ple_rstd, t + 1)
                        STT(emb[0:r, :], emb[0:r, :], st3[0:r, 3:4], pleg_b[0:r, :], ALU.mult, ALU.mult).then_inc(em2, 1)
                        dve.wait_ge(em2, t + 1)
                        dve.tensor_tensor(h3[0:r, :], h2[b][0:r, :], emb[0:r, :], ALU.add).then_inc(h3_ready, 1)
                        if r2:
                            dve.wait_ge(h3_ready, t + 1)
                            combine(t + 2, turn + 1, b, r2)
                        dve.wait_ge(h3_rstd, t + 1)
                        if not isinstance(t, int) or t > 0:
                            dve.wait_ge(out_stored, 16 * t)
                        STT(outb[0:r, :], h3[0:r, :], st3[0:r, 6:7], fing_b[0:r, :], ALU.mult, ALU.mult).then_inc(out_ready, 1)

                    dve.sem_inc(em1, 2)
                    for k in range(KD):
                        if k == KD - 2:
                            combine(0, 0, 0, P)
                        dve.wait_ge(w_scaled_act, W_IN_SHARE + k + 1)
                        dve.tensor_tensor(pg_lo[:, k, :], w_pg[:, k, :], pg_hi[:, k, :].bitcast(F32), ALU.subtract).then_inc(w_scaled, 1)
                    hT_half(0, 0, P)
                    combine(1, 0, 1, P)
                    tiles(tile)(dve)
    return nc


_INS = ["x_prompt", "x_sample", "state_C", "state_n", "state_m", "state_conv", "p_prompt", "p_sample", "norm_mix_g",
        "w_in", "conv_w", "conv_b", "b_igate", "b_fgate", "hnorm_g", "vnorm_g", "w_s", "b_s", "w_out", "norm_ffn_g",
        "router_g_w", "router_g_b", "router_e_w", "router_e_b", "w1", "w3", "w2", "w_ple", "ple_norm_g", "w_ple_gate",
        "final_norm_g"]
_OUTS = [("y_p", (1, SEQ, D)), ("y_s", (NS, 1, D)), ("C_p", (1, 1, H, P, P)), ("n_p", (1, 1, H, P)), ("m_p", (1, 1, H)),
         ("conv_p", (1, 1, CW - 1, QK)), ("C_s", (1, NS, H, P, P)), ("n_s", (1, NS, H, P)), ("m_s", (1, NS, H)),
         ("conv_s", (1, NS, CW - 1, QK)), ("v_s", (1, NS, 1, 512))]


def kernel(**inputs):
    import numpy as np
    import concourse.bacc as bacc
    from concourse.bass_utils import run_bass_kernel_spmd

    nc = bacc.Bacc("TRN2", target_bir_lowering=False, num_devices=1, dynamic_dma_scratch_size=12288)
    arrays, a, o = {}, {}, {}
    for name in _INS:
        v = np.ascontiguousarray(inputs[name])
        arrays[f"in_{name}"] = v
        a[name] = nc.dram_tensor(f"in_{name}", v.shape, mybir.dt.from_np(v.dtype), kind="ExternalInput").ap()
    for name, shape in _OUTS:
        o[name] = nc.dram_tensor(f"out_{name}", shape, F32, kind="ExternalOutput").ap()
    program(nc, a, o)
    r = run_bass_kernel_spmd(nc, [arrays], core_ids=[0])
    return tuple(r.results[0][f"out_{name}"] for name, _ in _OUTS)
```
